# Optimizing a Trainium2 kernel written in Bass

```python
import math
import jax, jax.numpy as jnp
from jax import lax
import numpy as np

D_MODEL = 2048
BATCH = 1
SEQ = 256
DEPTH = 2

CHUNK = 64
EPS = 1e-6
N_BRANCH = 3
BRANCH_WIDTH = D_MODEL // 2
S5_WIDTH = BRANCH_WIDTH
S5_GROUP = 16
S5_GROUPS = S5_WIDTH // S5_GROUP
S5_STATE = 64
S5_BLOCK = 128
SSD_INNER = BRANCH_WIDTH
SSD_HEAD_DIM = 64
SSD_HEADS = SSD_INNER // SSD_HEAD_DIM
SSD_GROUPS = 2
SSD_STATE = 128
SSD_CONV = 4
SSD_CONV_DIM = SSD_INNER + 2 * SSD_GROUPS * SSD_STATE
ATT_HEAD_DIM = 64
ATT_HEADS = BRANCH_WIDTH // ATT_HEAD_DIM
ATT_KV_HEADS = 4
ATT_REP = ATT_HEADS // ATT_KV_HEADS
ATT_WIDTH = ATT_HEADS * ATT_HEAD_DIM
ATT_KV_WIDTH = ATT_KV_HEADS * ATT_HEAD_DIM
WINDOW = 128
WINDOW_CHUNKS = WINDOW // CHUNK
ROT_DIM = ATT_HEAD_DIM // 4
ROPE_THETA = 500000.0
IN_SIZES = (S5_WIDTH, S5_WIDTH, SSD_INNER, SSD_CONV_DIM, SSD_HEADS,
            ATT_WIDTH, ATT_KV_WIDTH, ATT_KV_WIDTH, ATT_WIDTH, N_BRANCH * D_MODEL)
D_IN = sum(IN_SIZES)

kernel_name = "hybrid_s5_ssd_swa_gated_trunk"

def rmsnorm(t, w):
    t32 = t.astype(jnp.float32)
    y = t32 * lax.rsqrt(jnp.mean(t32 * t32, axis=-1, keepdims=True) + EPS)
    return (y * w.astype(jnp.float32)).astype(t.dtype)

def split_points():
    pts, acc = [], 0
    for s in IN_SIZES[:-1]:
        acc += s
        pts.append(acc)
    return pts

def s5_mixer(u, a_re, a_im, b_re, b_im, c_re, c_im, d, log_dt, w_glu, b_glu):
    bsz, L, _ = u.shape
    f32 = jnp.float32
    u32 = u.astype(f32)
    lam = lax.complex(a_re.astype(f32), a_im.astype(f32))
    dt = jnp.exp(log_dt.astype(f32))[:, None]
    lam_bar = jnp.exp(lam * dt)
    b_bar = ((lam_bar - 1.0) / lam)[..., None] * lax.complex(b_re.astype(f32), b_im.astype(f32))
    c = lax.complex(c_re.astype(f32), c_im.astype(f32))
    nb = L // S5_BLOCK
    ub = u32.reshape(bsz, nb, S5_BLOCK, S5_GROUPS, S5_GROUP).transpose(1, 0, 2, 3, 4)
    a_blk = jnp.broadcast_to(lam_bar, (bsz, S5_BLOCK, S5_GROUPS, S5_STATE))

    def binop(e1, e2):
        a1, b1 = e1
        a2, b2 = e2
        return a2 * a1, a2 * b1 + b2

    def step(carry, u_blk):
        bu = jnp.einsum('btgh,gph->btgp', u_blk.astype(jnp.complex64), b_bar)
        a_cum, s_loc = lax.associative_scan(binop, (a_blk, bu), axis=1)
        s = s_loc + a_cum * carry[:, None]
        y = jnp.einsum('btgp,ghp->btgh', s, c).real
        return s[:, -1], y

    init = jnp.zeros((bsz, S5_GROUPS, S5_STATE), jnp.complex64)
    _, ys = lax.scan(step, init, ub)
    y = ys.transpose(1, 0, 2, 3, 4).reshape(bsz, L, S5_WIDTH) + d.astype(f32) * u32
    y = jax.nn.gelu(y)
    return y * jax.nn.sigmoid(y @ w_glu.astype(f32) + b_glu.astype(f32))

def segsum(t):
    T = t.shape[-1]
    cs = jnp.cumsum(t, axis=-1)
    diff = cs[..., :, None] - cs[..., None, :]
    mask = jnp.tril(jnp.ones((T, T), dtype=bool))
    return jnp.where(mask, diff, -jnp.inf)

def ssd_mixer(z, xbc, dt_raw, conv_w, conv_b, dt_bias, a_log, d_skip, norm_w):
    f32 = jnp.float32
    bsz, L, _ = z.shape
    nc = L // CHUNK
    xbc = xbc.astype(f32)
    conv = lax.conv_general_dilated(xbc, conv_w.astype(f32)[:, None, :], window_strides=(1,),
                                    padding=[(SSD_CONV - 1, 0)],
                                    dimension_numbers=('NWC', 'WIO', 'NWC'),
                                    feature_group_count=SSD_CONV_DIM)
    xbc = jax.nn.silu(conv + conv_b.astype(f32))
    gn = SSD_GROUPS * SSD_STATE
    xs = xbc[..., :SSD_INNER].reshape(bsz, nc, CHUNK, SSD_HEADS, SSD_HEAD_DIM)
    rep = SSD_HEADS // SSD_GROUPS
    bm = jnp.repeat(xbc[..., SSD_INNER:SSD_INNER + gn].reshape(bsz, L, SSD_GROUPS, SSD_STATE), rep, axis=2)
    cm = jnp.repeat(xbc[..., SSD_INNER + gn:].reshape(bsz, L, SSD_GROUPS, SSD_STATE), rep, axis=2)
    bm = bm.reshape(bsz, nc, CHUNK, SSD_HEADS, SSD_STATE)
    cm = cm.reshape(bsz, nc, CHUNK, SSD_HEADS, SSD_STATE)
    dt = jax.nn.softplus(dt_raw.astype(f32) + dt_bias.astype(f32)).reshape(bsz, nc, CHUNK, SSD_HEADS)
    a = (dt * -jnp.exp(a_log.astype(f32))).transpose(0, 3, 1, 2)
    xdt = xs * dt[..., None]
    a_cum = jnp.cumsum(a, axis=-1)
    lmat = jnp.exp(segsum(a))
    scores = jnp.einsum('bclhn,bcshn->bhcls', cm, bm) * lmat
    y_diag = jnp.einsum('bhcls,bcshp->bclhp', scores, xdt)
    decay_states = jnp.exp(a_cum[..., -1:] - a_cum)
    states = jnp.einsum('bclhn,bhcl,bclhp->bchpn', bm, decay_states, xdt)
    states = jnp.concatenate([jnp.zeros_like(states[:, :1]), states], axis=1)
    chunk_decay = jnp.exp(segsum(jnp.pad(a_cum[..., -1], ((0, 0), (0, 0), (1, 0)))))
    new_states = jnp.einsum('bhzc,bchpn->bzhpn', chunk_decay, states)
    prev_states = new_states[:, :-1]
    y_off = jnp.einsum('bclhn,bchpn,bhcl->bclhp', cm, prev_states, jnp.exp(a_cum))
    y = y_diag + y_off + xs * d_skip.astype(f32)[:, None]
    y = y.reshape(bsz, L, SSD_INNER)
    return rmsnorm(y * jax.nn.silu(z.astype(f32)), norm_w)

def partial_rope(t, pos):
    half = ROT_DIM // 2
    inv = ROPE_THETA ** (-jnp.arange(half, dtype=jnp.float32) * 2.0 / ROT_DIM)
    ang = pos[:, None] * inv[None, :]
    cos = jnp.cos(ang)[None, :, None, :]
    sin = jnp.sin(ang)[None, :, None, :]
    t1 = t[..., :half]
    t2 = t[..., half:ROT_DIM]
    return jnp.concatenate([t1 * cos - t2 * sin, t1 * sin + t2 * cos, t[..., ROT_DIM:]], axis=-1)

def shift_chunks(t, s):
    if s == 0:
        return t
    pad = [(0, 0)] * t.ndim
    pad[1] = (s, 0)
    return jnp.pad(t, pad)[:, :t.shape[1]]

def window_attention(q, k, v, gate, q_norm_w, k_norm_w, sinks):
    f32 = jnp.float32
    bsz, L, _ = q.shape
    nc = L // CHUNK
    pos = jnp.arange(L, dtype=f32)
    q = rmsnorm(q.astype(f32).reshape(bsz, L, ATT_HEADS, ATT_HEAD_DIM), q_norm_w)
    k = rmsnorm(k.astype(f32).reshape(bsz, L, ATT_KV_HEADS, ATT_HEAD_DIM), k_norm_w)
    q = partial_rope(q, pos)
    k = partial_rope(k, pos)
    v = v.astype(f32).reshape(bsz, L, ATT_KV_HEADS, ATT_HEAD_DIM)
    qc = q.reshape(bsz, nc, CHUNK, ATT_KV_HEADS, ATT_REP, ATT_HEAD_DIM)
    kc = k.reshape(bsz, nc, CHUNK, ATT_KV_HEADS, ATT_HEAD_DIM)
    vc = v.reshape(bsz, nc, CHUNK, ATT_KV_HEADS, ATT_HEAD_DIM)
    shifts = range(WINDOW_CHUNKS - 1, -1, -1)
    kb = jnp.concatenate([shift_chunks(kc, s) for s in shifts], axis=2)
    vb = jnp.concatenate([shift_chunks(vc, s) for s in shifts], axis=2)
    src_chunk = (jnp.arange(nc)[:, None] - (WINDOW_CHUNKS - 1)
                 + jnp.arange(WINDOW_CHUNKS * CHUNK)[None, :] // CHUNK)
    valid = (src_chunk >= 0)[None, :, None, None, None, :]
    s = jnp.einsum('bcqgrd,bcsgd->bcgrqs', qc, kb) * (ATT_HEAD_DIM ** -0.5)
    s = jnp.where(valid, s, jnp.finfo(f32).min)
    sink = sinks.astype(f32).reshape(ATT_KV_HEADS, ATT_REP)[None, None, :, :, None, None]
    m = jnp.maximum(jnp.max(s, axis=-1, keepdims=True), sink)
    p = jnp.exp(s - m)
    denom = jnp.sum(p, axis=-1, keepdims=True) + jnp.exp(sink - m)
    o = jnp.einsum('bcgrqs,bcsgd->bcqgrd', p / denom, vb)
    return o.reshape(bsz, L, ATT_WIDTH) * jax.nn.silu(gate.astype(f32))

def setup_inputs(seed: int = 0) -> dict:
    key = jax.random.key(seed)
    ks = jax.random.split(key, 24)
    f32 = jnp.float32

    def nrm(k, shape, scale):
        return jax.random.normal(k, shape, f32) * scale

    G, P = S5_GROUPS, S5_STATE
    x = nrm(ks[0], (BATCH, SEQ, D_MODEL), 1.0)
    norm_w = 1.0 + nrm(ks[1], (DEPTH, D_MODEL), 0.01)
    w_in = nrm(ks[2], (DEPTH, D_MODEL, D_IN), D_MODEL ** -0.5)
    s5_a_re = -0.5 + nrm(ks[3], (DEPTH, G, P), 0.01)
    s5_a_im = jnp.broadcast_to(math.pi * jnp.arange(P, dtype=f32), (DEPTH, G, P))
    s5_b_re = nrm(ks[4], (DEPTH, G, P, S5_GROUP), (2 * S5_GROUP) ** -0.5)
    s5_b_im = nrm(ks[5], (DEPTH, G, P, S5_GROUP), (2 * S5_GROUP) ** -0.5)
    s5_c_re = nrm(ks[6], (DEPTH, G, S5_GROUP, P), (2 * P) ** -0.5)
    s5_c_im = nrm(ks[7], (DEPTH, G, S5_GROUP, P), (2 * P) ** -0.5)
    s5_d = nrm(ks[8], (DEPTH, S5_WIDTH), 1.0)
    s5_log_dt = jax.random.uniform(ks[9], (DEPTH, G), f32, math.log(1e-3), math.log(1e-1))
    s5_w_glu = nrm(ks[10], (DEPTH, S5_WIDTH, S5_WIDTH), S5_WIDTH ** -0.5)
    s5_b_glu = nrm(ks[11], (DEPTH, S5_WIDTH), 0.01)
    ssd_conv_w = nrm(ks[12], (DEPTH, SSD_CONV, SSD_CONV_DIM), SSD_CONV ** -0.5)
    ssd_conv_b = nrm(ks[13], (DEPTH, SSD_CONV_DIM), 0.01)
    dt0 = jnp.exp(jax.random.uniform(ks[14], (DEPTH, SSD_HEADS), f32, math.log(1e-3), math.log(1e-1)))
    ssd_dt_bias = dt0 + jnp.log(-jnp.expm1(-dt0))
    ssd_a_log = jnp.log(jax.random.uniform(ks[15], (DEPTH, SSD_HEADS), f32, 1.0, 16.0))
    ssd_d = 1.0 + nrm(ks[16], (DEPTH, SSD_HEADS), 0.01)
    ssd_norm_w = 1.0 + nrm(ks[17], (DEPTH, SSD_INNER), 0.01)
    att_q_norm = 1.0 + nrm(ks[18], (DEPTH, ATT_HEAD_DIM), 0.01)
    att_k_norm = 1.0 + nrm(ks[19], (DEPTH, ATT_HEAD_DIM), 0.01)
    att_sinks = nrm(ks[20], (DEPTH, ATT_HEADS), 0.5)
    w_branch = nrm(ks[21], (DEPTH, N_BRANCH, BRANCH_WIDTH, D_MODEL), BRANCH_WIDTH ** -0.5)
    w_out = nrm(ks[22], (DEPTH, D_MODEL, D_MODEL), D_MODEL ** -0.5)
    return {"x": x, "norm_w": norm_w, "w_in": w_in,
            "s5_a_re": s5_a_re, "s5_a_im": s5_a_im, "s5_b_re": s5_b_re, "s5_b_im": s5_b_im,
            "s5_c_re": s5_c_re, "s5_c_im": s5_c_im, "s5_d": s5_d, "s5_log_dt": s5_log_dt,
            "s5_w_glu": s5_w_glu, "s5_b_glu": s5_b_glu,
            "ssd_conv_w": ssd_conv_w, "ssd_conv_b": ssd_conv_b, "ssd_dt_bias": ssd_dt_bias,
            "ssd_a_log": ssd_a_log, "ssd_d": ssd_d, "ssd_norm_w": ssd_norm_w,
            "att_q_norm": att_q_norm, "att_k_norm": att_k_norm, "att_sinks": att_sinks,
            "w_branch": w_branch, "w_out": w_out}

def reference(x, norm_w, w_in, s5_a_re, s5_a_im, s5_b_re, s5_b_im, s5_c_re, s5_c_im, s5_d,
              s5_log_dt, s5_w_glu, s5_b_glu, ssd_conv_w, ssd_conv_b, ssd_dt_bias, ssd_a_log,
              ssd_d, ssd_norm_w, att_q_norm, att_k_norm, att_sinks, w_branch, w_out):
    bsz, L, _ = x.shape
    pts = split_points()
    for i in range(DEPTH):
        h = rmsnorm(x, norm_w[i])
        proj = h @ w_in[i]
        (u, s5_gate, z, xbc, dt_raw, q, k, v, att_gate,
         merge_logits) = jnp.split(proj, pts, axis=-1)
        y_s5 = s5_mixer(u, s5_a_re[i], s5_a_im[i], s5_b_re[i], s5_b_im[i], s5_c_re[i], s5_c_im[i],
                        s5_d[i], s5_log_dt[i], s5_w_glu[i], s5_b_glu[i])
        y_s5 = y_s5 * jax.nn.silu(s5_gate.astype(jnp.float32))
        y_ssd = ssd_mixer(z, xbc, dt_raw, ssd_conv_w[i], ssd_conv_b[i], ssd_dt_bias[i],
                          ssd_a_log[i], ssd_d[i], ssd_norm_w[i])
        y_att = window_attention(q, k, v, att_gate, att_q_norm[i], att_k_norm[i], att_sinks[i])
        ys = jnp.stack([y_s5.astype(x.dtype), y_ssd.astype(x.dtype), y_att.astype(x.dtype)], axis=2)
        branches = jnp.einsum('blnw,nwd->blnd', ys, w_branch[i])
        gates = jax.nn.sigmoid(merge_logits.astype(jnp.float32)).reshape(bsz, L, N_BRANCH, D_MODEL)
        merged = jnp.sum(gates * branches.astype(jnp.float32), axis=2).astype(x.dtype)
        x = x + merged @ w_out[i]
    return x


_drawn_inputs = setup_inputs


def setup_inputs(seed=0):
    import zlib

    import numpy as np

    out = dict(_drawn_inputs(seed))
    spreads = {}
    factors = {'norm_w': 5.033,
     's5_a_re': 64.0,
     's5_a_im': 56.4,
     's5_b_re': 64.0,
     's5_b_im': 64.0,
     's5_c_re': 64.0,
     's5_c_im': 64.0,
     's5_log_dt': 57.296,
     's5_b_glu': 8.0,
     'ssd_conv_b': 6.381,
     'ssd_d': 64.0,
     'ssd_norm_w': 8.0,
     'att_q_norm': 8.0,
     'att_k_norm': 8.0,
     'att_sinks': 8.0}
    for name, (base, spread) in spreads.items():
        noise = np.random.default_rng([zlib.crc32(name.encode()), seed]).standard_normal(out[name].shape)
        drawn = base * np.exp(spread * noise) if base else spread * noise
        out[name] = __import__('jax').numpy.asarray(drawn.astype(out[name].dtype))
    for name, factor in factors.items():
        out[name] = (out[name] * factor).astype(out[name].dtype)
    return out
```

```python
import math
from contextlib import ExitStack

import numpy as np

import concourse.bass as bass
from concourse import mybir

F32 = mybir.dt.float32
F32R = mybir.dt.float32r
ALU = mybir.AluOpType
ACT = mybir.ActivationFunctionType
AX = mybir.AxisListType

P = 128
D_MODEL, TOK, DEPTH = 2048, 256, 2
KT = D_MODEL // P
BW = D_MODEL // 2
BT = BW // P
S5_GROUPS, S5_GROUP, S5_STATE = 64, 16, 64
ST = S5_GROUPS * S5_STATE // P
HEADS, KV_HEADS, HD = 16, 4, 64
CONV = 4
EPS = 1e-6

PAIR = 2048
RAW, SPLIT = 2, 2
N_BC, N_KV, N_IN, N_GATE = 0, 4, 8, 56
N_GLU, N_BR, N_OUT, N_LAYER = 104, 108, 132, 148

U, SG, Z, XS, Q, AG, BC = 0, 8, 16, 24, 32, 40, 48
NSLOT = 52

PP = {}
_at = 0
for _n, _w in (("a_re", ST), ("a_im", ST), ("log_dt", ST), ("s5_d", BT), ("b_glu", BT), ("conv", 12 * 5),
               ("ssd_norm", BT), ("ssd_d", BT), ("q_norm", 1), ("k_norm", 1), ("dt_bias", 16), ("a_log", 16),
               ("sinks", 16), ("w_dt", KT * 16), ("c_re", ST * 16), ("c_im", ST * 16)):
    PP[_n] = (_at, _w)
    _at += _w
NPP = _at

CC = {}
_at = 0
for _n, _w in (("tri", TOK), ("strict", P), ("ident", P), ("ones", P), ("blk", P), ("rot", P), ("amask", 384),
               ("cos", TOK), ("sin", TOK), ("iota", TOK), ("bmask", 8), ("half_pi", 1)):
    CC[_n] = (_at, _w)
    _at += _w
NCC = _at

TWO_PI = 6.2831850
INV_2PI = 1.0 / (2.0 * math.pi)
C1 = 6.28125
C2 = 0.0019340515136718750
C3 = 2.0 * math.pi - C1 - C2
ROUND = 12582912.0
GELU = math.sqrt(2.0 / math.pi)


def constants():
    c = np.zeros((P, NCC), np.float32)
    k = np.arange(P)

    def put(name, a):
        at, w = CC[name]
        c[:, at:at + w] = np.asarray(a, np.float32).reshape(P, w)

    put("tri", np.concatenate([(k[:, None] <= k[None, :]), np.ones((P, P))], 1))
    put("strict", k[:, None] > k[None, :])
    put("ident", np.eye(P))
    put("ones", np.ones((P, P)))
    put("blk", (k[:, None] // HD) == (k[None, :] // HD))
    rot = np.zeros((P, P))
    half = HD // 8
    for h in (0, HD):
        for i in range(half):
            rot[h + half + i, h + i] = -1.0
            rot[h + i, h + half + i] = 1.0
    put("rot", rot)
    q = k // 64
    m = np.full((P, 384), -1e30)
    key0 = np.arange(128) // 64
    m[:, :128][(key0[None, :] <= q[:, None]) & (key0[None, :] >= q[:, None] - 1)] = 0.0
    key1 = np.arange(256) // 64
    m[:, 128:][(key1[None, :] <= q[:, None] + 2) & (key1[None, :] >= q[:, None] + 1)] = 0.0
    put("amask", m)
    inv = (np.float32(500000.0) ** (-np.arange(half, dtype=np.float32) * np.float32(2.0) / np.float32(HD // 4))).astype(np.float32)
    ang = (np.arange(TOK, dtype=np.float32)[:, None] * inv[None, :]).astype(np.float32).astype(np.float64)
    cos, sin = np.ones((P, TOK)), np.zeros((P, TOK))
    for h in (0, HD):
        for i in range(half):
            for r in (h + i, h + half + i):
                cos[r], sin[r] = np.cos(ang[:, i]), np.sin(ang[:, i])
    put("cos", cos)
    put("sin", sin)
    put("iota", np.broadcast_to(np.arange(TOK), (P, TOK)))
    put("bmask", (k[:, None] // S5_GROUP) == np.arange(8)[None, :])
    put("half_pi", np.full((P, 1), math.pi / 2))
    return c


class Steps:

    def __init__(self, sem, names):
        self.sem, self.names, self.seen = sem, names, []

    def mark(self, ins, name):
        self.seen.append(name)
        ins.then_inc(self.sem, 1)
        return ins

    @property
    def n(self):
        return len(self.names) if self.names else 1

    def place(self, name):
        return self.names.index(name) + 1 if self.names else 1


def program(nc, x, norm_w, params, consts, bdense, stream, xs_out, order):
    with ExitStack() as ctx:
        def sem(name):
            return ctx.enter_context(nc.semaphore(name))

        base = (nc.sbuf_base + 31) // 32 * 32
        top = [base]

        def at(name, shape, dt, offset):
            return nc.alloc_sbuf_tensor_at(name, shape, dt, offset=offset)

        def sb(name, shape, dt=F32):
            n = 4
            for d in shape[1:]:
                n *= d
            o = top[0]
            top[0] += (n + 31) // 32 * 32
            return at(name, shape, dt, o)

        raw = sb("raw", [P, RAW, PAIR])
        w_hi = sb("w_hi", [P, SPLIT, PAIR], F32R)
        w_lo = sb("w_lo", [P, SPLIT, PAIR], F32R)
        h_hi = sb("h_hi", [P, KT, TOK], F32R)
        h_lo = sb("h_lo", [P, KT, TOK], F32R)
        o_proj = top[0]
        proj = sb("proj", [P, NSLOT, TOK])
        ys = at("ys", [P, NSLOT, TOK], F32R, o_proj)
        cst = sb("cst", [P, NCC])
        par = sb("par", [P, NPP])
        nw = sb("nw", [P, DEPTH, KT])
        kt = sb("kt", [P, 2, TOK])
        vt = sb("vt", [P, 2, TOK])
        rstd = sb("rstd", [P, TOK])
        rtok = sb("rtok", [P, 2])
        gm = sb("gm", [P, 2, 384])
        s5p = sb("s5p", [P, 4, ST])
        turn_hi = sb("turn_hi", [P, ST], F32R)
        dta = sb("dta", [P, 2, 2, 16])
        bgh = sb("bgh", [P, BT])
        work = top[0]
        tab = sb("tab", [P, 2, 2, TOK])
        prod = sb("prod", [P, 2, 2, TOK])
        prod2 = sb("prod2", [P, 2, TOK])
        wst = sb("wst", [P, 2, TOK])
        frac = sb("frac", [P, 2, TOK])
        tA = sb("tA", [P, TOK])
        tB = sb("tB", [P, TOK])
        zabs = sb("zabs", [P, TOK])
        bz = sb("bz", [P, 2, 8, 64])
        cz = sb("cz", [P, 4, 2, 32])
        bd = sb("bd", [P, 2, 2 * 64])
        cur = sb("cur", [P, 2, 48])
        xc = sb("xc", [P, TOK])
        tt = sb("tt", [P, TOK])
        xdt = sb("xdt", [P, 2, 2, 64])
        m1 = sb("m1", [P, 3, P])
        ex = sb("ex", [P, 384])
        stt_ = sb("stt", [P, 384])
        sc = sb("sc", [P, 384])
        pr = sb("pr", [P, 384])
        pt = sb("pt", [P, 384])
        qn = sb("qn", [P, TOK])
        qh = sb("qh", [P, TOK])
        rq = sb("rq", [P, TOK])
        rv = sb("rv", [P, TOK])
        y5 = sb("y5", [P, TOK])
        kcur = sb("kcur", [P, TOK])
        vcur = sb("vcur", [P, 2, 64])
        small = sb("small", [P, 16])
        gt = sb("gt", [P, 4, TOK])
        end = top[0]
        w0 = [work]

        def al(name, shape, dt=F32):
            n = 4
            for d in shape[1:]:
                n *= d
            o = w0[0]
            w0[0] += (n + 31) // 32 * 32
            assert w0[0] <= end
            return at(name, shape, dt, o)

        sp = al("sp", [P, 12, ST])
        cw = al("cw", [P, 2, ST * 16])
        wdt_hi = al("wdt_hi", [P, KT, 16], F32R)
        wdt_lo = al("wdt_lo", [P, KT, 16], F32R)
        sd = al("sd", [P, 8, 32])
        kk = al("kk", [P, 4, 2 * TOK])
        bt = al("bt", [P, TOK])
        sv = al("sv", [P, 2, TOK])
        w0[0] = work
        g2_hi = al("g2_hi", [P, BT, TOK], F32R)
        g2_lo = al("g2_lo", [P, BT, TOK], F32R)
        nrm = al("nrm", [P, 2, TOK])
        ssq = al("ssq", [P, 2, 2 * TOK])
        tg = al("tg", [P, 2, 2, TOK])
        gin = al("gin", [P, 2, 2, TOK])
        acc = al("acc", [P, 2, TOK])
        tmp = al("tmp", [P, TOK])
        tmph = al("tmph", [P, 2, TOK])
        assert end <= nc.sbuf_usable_end

        mm = ctx.enter_context(nc.psum_tensor("mm", [P, 2, 512], F32))
        bs = ctx.enter_context(nc.psum_tensor("bs", [P, 512], F32))
        by = ctx.enter_context(nc.psum_tensor("by", [P, 512], F32))
        b4 = ctx.enter_context(nc.psum_tensor("b4", [P, 512], F32))
        b5 = ctx.enter_context(nc.psum_tensor("b5", [P, 512], F32))
        b6 = ctx.enter_context(nc.psum_tensor("b6", [P, 512], F32))
        b7 = ctx.enter_context(nc.psum_tensor("b7", [P, 512], F32))
        ps_s5 = bs[:, 0:256]
        ps_ssd = by[:, 0:256]
        ps_att = by[:, 256:512]

        gscr = nc.dram_tensor("gscr", [3 * KT, P, TOK], F32)
        kscr = nc.dram_tensor("kscr", [2, P, TOK], F32)

        landed = [sem(f"landed{i}") for i in range(RAW)]
        hi_done = sem("hi_done")
        lo_done = sem("lo_done")
        pair_done = sem("pair_done")
        spilled = [sem(f"spilled{i}") for i in range(4)]
        const_in = sem("const_in")
        x_in = sem("x_in")
        x_copied = sem("x_copied")
        par_in = sem("par_in")
        k_out = sem("k_out")
        k_in = sem("k_in")
        b_in = sem("b_in")
        gate_in = [sem(f"gate_in{i}") for i in range(2)]
        x_back = sem("x_back")
        x_out = sem("x_out")
        passed = sem("passed")
        merged = sem("merged")
        merged_hi = sem("merged_hi")
        merged_lo = sem("merged_lo")
        summed = sem("summed")

        steps = {}
        for kind in ("L", "M"):
            for e in "PVAG":
                s = Steps(sem({"P": "pe", "V": "vec", "A": "act", "G": "pool"}[e] + {"L": "_layer", "M": "_mix"}[kind]),
                          None if order is None else order[kind + e])
                steps[kind + e] = s
        LP, LV, LA, LG = (steps["L" + e] for e in "PVAG")
        MP, MV, MA, MG = (steps["M" + e] for e in "PVAG")

        def C(name, w=None):
            a, n = CC[name]
            return cst[:, a:a + (w or n)]

        def PR(name, a=0, n=1):
            o = PP[name][0] + a
            return par[:, o:o + n]

        class Where:

            def __init__(self, e):
                self.e, self.b = e, {}

            def layer(self, L):
                for s in (LP, LV, LA, LG):
                    self.b[s] = self.e.snap((L + 2) * s.n)

            def tile(self, L, I, c):
                for s in (MP, MV, MA, MG):
                    self.b[s] = self.e.snap((L * 8 + I * 2 + (c + 2)) * s.n)

            def last_tile(self, L):
                for s in (MP, MV, MA, MG):
                    self.b[s] = self.e.snap((L * 8 + 9) * s.n)

            def wait(self, s, name, back=0):
                self.e.wait_ge(s.sem, self.b[s] + (s.place(name) - back * s.n))

            def settle(self):
                self.e.sem_inc(passed, 1)

        block = ctx.enter_context(nc.Block())

        @block.sync
        def _(e):
            e.dma_start(cst[:], consts).then_inc(const_in, 16)
            e.dma_start(nw[:], norm_w).then_inc(const_in, 16)
            e.dma_start(proj[:, 0:KT, :], x).then_inc(x_in, 16)
            with e.Fori(0, DEPTH) as L:
                with e.Fori(0, N_LAYER // RAW) as I:
                    nb = e.snap(L * N_LAYER + I * RAW)
                    for j in range(RAW):
                        e.wait_ge(lo_done, nb + (j + 1))
                        e.dma_start(raw[:, j, :], stream[nb + j]).then_inc(landed[j], 16)
            for j in range(2):
                e.wait_ge(lo_done, DEPTH * N_LAYER + j + 1)
                e.dma_start(raw[:, j, :], stream[j]).then_inc(landed[j], 16)
            e.wait_ge(x_out, (DEPTH + 1) * 64)
            e.wait_ge(x_copied, 16)

        @block.gpsimd
        def _(e):
            W = Where(e)
            e.sem_inc(LG.sem, 2 * LG.n)
            e.sem_inc(MG.sem, 2 * MG.n)
            e.sem_inc(x_out, 64)
            e.dma_start(xs_out[0], x).then_inc(x_copied, 16)
            with e.Fori(0, DEPTH) as L:
                W.layer(L)
                lw = e.snap(L * N_LAYER + RAW + 2)
                e.wait_ge(lo_done, lw)
                W.settle()
                e.dma_start(par[:], params[L]).then_inc(par_in, 16)
                e.wait_ge(lo_done, lw)
                W.wait(LV, "prep_end")
                W.wait(LA, "prep_end")
                W.wait(LP, "k_rot")
                W.settle()
                LG.mark(e.memset(cz[:], 0.0), "cz0")
                W.wait(LG, "cz0")
                kin = e.snap(L * 32 + 32)
                W.settle()
                with e.Fori(0, 4) as I:
                    for c in range(2):
                        W.tile(L, I, c)
                        i = I * 2 + c
                        W.wait(MV, "end", 2)
                        W.wait(MA, "end", 2)
                        W.wait(MG, "end", 1)
                        e.wait_ge(const_in, 32)
                        cc = cur[:, c, :]
                        MG.mark(e.tensor_copy(cc[:, 0:16].rearrange("p (a b) -> p a b", a=4),
                                              s5p[:, :, bass.ds(i * 4, 4)]), "cur0")
                        MG.mark(e.tensor_copy(cc[:, 16:24].rearrange("p (a b d) -> p a b d", a=2, b=2),
                                              dta[:, :, :, bass.ds(i * 2, 2)]), "cur1")
                        MG.mark(e.tensor_copy(cc[:, 24:26], par[:, bass.ds(i * 2 + PP["sinks"][0], 2)]), "cur2")
                        MG.mark(e.tensor_copy(cc[:, 26:27], par[:, bass.ds(i + PP["s5_d"][0], 1)]), "cur3")
                        MG.mark(e.tensor_copy(cc[:, 27:28], par[:, bass.ds(i + PP["ssd_d"][0], 1)]), "cur4a")
                        MG.mark(e.tensor_copy(cc[:, 28:33], par[:, bass.ds(i * 5 + PP["conv"][0], 5)]), "cur5")
                        W.wait(MG, "cur4a")
                        W.settle()
                        MG.mark(e.tensor_scalar(cc[:, 27:28], cc[:, 27:28], 0.5, 0.0, ALU.mult, ALU.add), "cur4")
                        e.dma_start(bd[:, c, :], bdense[L, i]).then_inc(b_in, 16)

                        def turns(j):
                            if j < 2:
                                W.wait(MA, f"cos{j + 2}", 1)
                            else:
                                W.wait(MA, f"cos{j - 2}")
                            W.wait(MG, f"frac{j - 1}" if j else "cur0")
                            W.settle()
                            MG.mark(e.tensor_scalar(tA[:], C("iota"), cc[:, 4 + j:5 + j], ROUND, ALU.mult, ALU.add), f"ta{j}")
                            W.settle()
                            MG.mark(e.tensor_scalar(tB[:], C("iota"), cc[:, 8 + j:9 + j], 0.0, ALU.mult, ALU.add), f"tb{j}")
                            W.wait(MG, f"ta{j}")
                            W.settle()
                            MG.mark(e.tensor_scalar(tA[:], tA[:], -ROUND, 1.0, ALU.add, ALU.mult), f"tc{j}")
                            W.wait(MG, f"tc{j}")
                            MG.mark(e.tensor_tensor(tB[:], tB[:], tA[:], ALU.subtract), f"td{j}")
                            W.wait(MG, f"td{j}")
                            W.settle()
                            MG.mark(e.tensor_scalar(tA[:], C("iota"), cc[:, 12 + j:13 + j], 0.0, ALU.mult, ALU.add), f"te{j}")
                            W.wait(MG, f"te{j}")
                            MG.mark(e.tensor_tensor(tB[:], tB[:], tA[:], ALU.add), f"tf{j}")
                            W.wait(MG, f"tf{j}")
                            W.settle()
                            MG.mark(e.tensor_scalar(frac[:, j % 2, :], tB[:], 0.5, -0.5, ALU.min, ALU.max), f"frac{j}")

                        turns(0)
                        turns(1)
                        bval = e.snap((L * 8 + i + 1) * 16)
                        e.wait_ge(b_in, bval)
                        W.wait(MP, "bu3", 1)
                        for r in range(2):
                            MG.mark(e.tensor_tensor(bz[:, r], bd[:, c, r * 64:r * 64 + 64].unsqueeze(1).broadcast_to([P, 8, 64]),
                                                    C("bmask").unsqueeze(2).broadcast_to([P, 8, 64]), ALU.mult), f"bz{r}")
                        W.wait(MP, "C3", 1)
                        for g in range(2):
                            rows = slice(64 * g, 64 * g + 64)
                            for r, nm in enumerate(("c_re", "c_im")):
                                o = PP[nm][0]
                                W.wait(MG, "bz1" if (g, r) == (0, 0) else f"cz{g}0" if r else "cz01")
                                MG.mark(e.tensor_copy(cz[rows, :, r, 16 * g:16 * g + 16],
                                                      par[rows, bass.ds(i * 64 + o, 64)].rearrange("p (j h) -> p j h", j=4)), f"cz{g}{r}")
                        W.wait(MG, "cz11")
                        if c == 0:
                            W.wait(MP, "A3_1", 1)
                            for r in range(2):
                                e.wait_ge(k_out, e.snap((L + 1) * 16))
                                W.settle()
                                e.dma_start(kcur[64 * r:64 * r + 64, :],
                                            kscr.rearrange("a (b p) t -> (a b) p t", b=2)[I]).then_inc(k_in, 16)
                            MG.mark(e.tensor_copy(vcur[:], vt[:, :, bass.ds(I * 64, 64)]), "vcur")
                        else:
                            W.settle()
                            MG.mark(e.memset(small[:, 15:16], 0.0), "vcur")
                        turns(2)
                        turns(3)
                        W.settle()
                        MG.mark(e.memset(small[:, 14:15], 0.0), "end")
                e.wait_ge(pair_done, e.snap(L * N_LAYER + N_OUT + SPLIT))
                e.wait_ge(x_copied, 16)
                e.wait_ge(x_out, e.snap((L + 1) * 64))
                W.settle()
                e.dma_start(proj[:, 16:32, :], xs_out[L]).then_inc(x_back, 16)

        @block.scalar
        def _(e):
            W = Where(e)
            e.sem_inc(LA.sem, 2 * LA.n)
            e.sem_inc(MA.sem, 2 * MA.n)
            e.sem_inc(merged_hi, 2)
            for s in spilled:
                e.sem_inc(s, 16)

            def hi(nb, j):
                if isinstance(nb, int):
                    e.wait_ge(landed[j % RAW], 16 * (j // RAW + 1))
                    e.wait_ge(pair_done, nb + (j + 1))
                else:
                    e.wait_ge(landed[j % RAW], nb[1] + 16 * (j // RAW))
                    e.wait_ge(pair_done, nb[0] + (j + 1))
                e.activation(w_hi[:, j % SPLIT, :], raw[:, j % RAW, :], ACT.Copy).then_inc(hi_done, 1)

            def start(L, off, I=None, g=0):
                n = L * N_LAYER + off if I is None else L * N_LAYER + I * g + off
                m = (L * (N_LAYER // RAW) + (off // RAW + 1)) * 16 if I is None else \
                    (L * (N_LAYER // RAW) + I * (g // RAW) + (off // RAW + 1)) * 16
                return e.snap(n), e.snap(m)

            hi(0, 0)
            hi(0, 1)
            with e.Fori(0, DEPTH) as L:
                W.layer(L)
                lw = e.snap(L * N_LAYER + RAW + 2)
                e.wait_ge(lo_done, lw)
                e.wait_ge(x_in, 16)
                for q in range(4):
                    LA.mark(e.activation(proj[:, 16 + 4 * q:20 + 4 * q, :], proj[:, 4 * q:4 * q + 4, :], ACT.Square), f"xsq{q}")
                for q in range(4):
                    W.wait(LV, f"xw{q}")
                    LA.mark(e.activation(h_hi[:, 4 * q:4 * q + 4, :], proj[:, 32 + 4 * q:36 + 4 * q, :], ACT.Copy), f"xhi{q}")
                W.wait(LV, "rs_v")
                LA.mark(e.activation(sv[:, 1, :], sv[:, 0, :], ACT.Sqrt), "rs_sqrt")
                W.wait(LV, "rt_v")
                LA.mark(e.activation(small[:, 4:6], small[:, 2:4], ACT.Sqrt), "rt_sqrt")
                pin = e.snap((L + 1) * 16)
                e.wait_ge(par_in, pin)
                LA.mark(e.activation(sp[:, 0, :], PR("log_dt", 0, ST), ACT.Exp), "s5_dt")
                W.wait(LV, "s5_ax")
                LA.mark(e.activation(sp[:, 2, :], sp[:, 1, :], ACT.Tanh, scale=0.5), "s5_tanh")
                LA.mark(e.activation(wdt_hi[:], PR("w_dt", 0, KT * 16).rearrange("p (k c) -> p k c", k=KT), ACT.Copy), "wdt_hi")
                LA.mark(e.activation(sd[:, 6, 0:16], PR("a_log", 0, 16), ACT.Exp), "exp_a")
                LA.mark(e.activation(bgh[:], PR("b_glu", 0, BT), ACT.Copy, scale=0.5), "bgh")
                W.wait(LV, "turn_abs")
                LA.mark(e.activation(sp[:, 5, :], sp[:, 3, :], ACT.Sin, scale=TWO_PI / 2), "s5_sin")
                LA.mark(e.activation(sp[:, 6, :], sp[:, 4, :], ACT.Sin, scale=-TWO_PI / 2, bias=C("half_pi")), "s5_cos")
                nb = start(L, 0)
                for j in range(8):
                    hi(nb, j + 2)
                W.wait(LV, "dt_abs")
                LA.mark(e.activation(sd[:, 2, :], sd[:, 1, :], ACT.Exp, scale=-1.0), "dt_exp")
                W.wait(LV, "k_raw")
                LA.mark(e.activation(kk[:, 0, :], kt[:].rearrange("p a b -> p (a b)"), ACT.Square), "k_sq")
                for t in range(4):
                    W.wait(LV, f"bc_conv{t}_3")
                    if t:
                        W.wait(LV, f"bc_silu{t - 1}")
                    LA.mark(e.activation(bt[:], kk[:, 2, 0:TOK] if t % 2 == 0 else kk[:, 2, TOK:], ACT.Tanh, scale=0.5), f"bc_tanh{t}")
                W.wait(LV, "k_v")
                LA.mark(e.activation(kk[:, 1, :], kk[:, 3, :], ACT.Sqrt), "k_sqrt")
                W.wait(LV, "k_fin")
                e.dma_start(kscr.rearrange("a p t -> p a t"), kt[:]).then_inc(k_out, 16)
                LA.mark(e.activation(small[:, 12:13], C("half_pi"), ACT.Copy), "prep_end")
                with e.Fori(0, 12) as I:
                    nb = start(L, N_IN, I, 4)
                    for j in range(4):
                        hi(nb, j + 2)

                with e.Fori(0, 4) as I:
                    nb = start(L, N_GATE, I, 12)
                    g0 = e.snap(I * 12)
                    for c in range(2):
                        W.tile(L, I, c)
                        i = I * 2 + c
                        cc = cur[:, c, :]
                        for t in range(6):
                            s = 6 * c + t
                            hi(nb, s + 2)
                            W.wait(MV, f"gt{t}")
                            MA.mark(e.activation(gt[:, s % 4, :], gt[:, s % 4, :], ACT.Tanh, scale=0.5), f"gate{t}")
                            W.wait(MA, f"gate{t}")
                            e.dma_start(gscr[g0 + s], gt[:, s % 4, :]).then_inc(spilled[s % 4], 16)

                            def sines(j):
                                W.wait(MG, f"frac{j}")
                                W.wait(MV, f"q2_{j + 2}" if j < 2 else f"q2_{j - 2}", 1 if j < 2 else 0)
                                MA.mark(e.activation(tab[:, j % 2, 1, :], frac[:, j % 2, :], ACT.Sin, scale=TWO_PI), f"sin{j}")
                                W.wait(MA, f"cos{j - 1}" if j else "cos3", 0 if j else 1)
                                MA.mark(e.activation(zabs[:], frac[:, j % 2, :], ACT.Abs), f"abs{j}")
                                W.wait(MA, f"abs{j}")
                                MA.mark(e.activation(tab[:, j % 2, 0, :], zabs[:], ACT.Sin, scale=-TWO_PI, bias=C("half_pi")), f"cos{j}")

                            def head_exp(h):
                                W.wait(MP, f"diff{h}")
                                W.wait(MV, "ST1" if h == 0 else "ST0", 1 if h == 0 else 0)
                                MA.mark(e.activation(ex[:], b6[:, 0:384], ACT.Exp), f"ex{h}")

                            def att_exp(h):
                                W.wait(MV, f"nm{h}")
                                if h:
                                    W.wait(MP, "A2_0")
                                else:
                                    W.wait(MP, "A2_1", 1)
                                MA.mark(e.activation(pr[:, 0:128], sc[:, 0:128], ACT.Exp, bias=small[:, 2:3],
                                                     accum_out=small[:, 4:5]), f"pe0{h}")
                                MA.mark(e.activation(pr[:, 128:384], sc[:, 128:384], ACT.Exp, bias=small[:, 3:4],
                                                     accum_out=small[:, 5:6]), f"pe1{h}")
                                MA.mark(e.activation(small[:, 6:8], small[:, 2:4], ACT.Exp, bias=cc[:, 24 + h:25 + h]), f"pes{h}")

                            def pt_out(h):
                                W.wait(MP, f"A2_{h}")
                                W.wait(MP, "A3_0" if h else "A3_1", 0 if h else 1)
                                MA.mark(e.activation(pt[:], b5[:, 0:384], ACT.Copy), f"pt{h}")

                            if t == 0:
                                W.wait(MV, "conv3")
                                W.wait(MV, "s5g2", 1)
                                MA.mark(e.activation(tt[:], xc[:], ACT.Tanh, scale=0.5), "xc_tanh")
                                W.wait(MV, "xc")
                                MA.mark(e.activation(tt[:], proj[:, bass.ds(i + Q, 1), :], ACT.Square), "q_sq")
                                W.wait(MV, "q_v")
                                MA.mark(e.activation(rq[:], rv[:], ACT.Sqrt), "q_sqrt")
                                sines(0)
                                sines(1)
                            if t == 1:
                                sines(2)
                                sines(3)
                            if t == 2:
                                head_exp(0)
                                att_exp(0)
                            if t == 3:
                                pt_out(0)
                                head_exp(1)
                                att_exp(1)
                            if t == 4:
                                pt_out(1)
                                W.wait(MP, "q_ss")
                                MA.mark(e.activation(qn[:], proj[:, bass.ds(i + Z, 1), :], ACT.Tanh, scale=0.5), "tz")
                                MA.mark(e.activation(rq[:], proj[:, bass.ds(i + AG, 1), :], ACT.Tanh, scale=0.5), "ta")
                                MA.mark(e.activation(rv[:], proj[:, bass.ds(i + SG, 1), :], ACT.Tanh, scale=0.5), "ts")
                                W.wait(MV, "y5")
                                MA.mark(e.activation(tt[:], y5[:], ACT.Square), "y5sq")
                            if t == 5:
                                W.wait(MV, "g5b")
                                MA.mark(e.activation(tt[:], tt[:], ACT.Tanh, scale=GELU), "g5t")
                                W.wait(MV, "yatt")
                                W.settle()
                                MA.mark(e.activation(ys[:, bass.ds(i + AG, 1), :], proj[:, bass.ds(i + Q, 1), :], ACT.Copy), "end")

                W.last_tile(L)
                W.wait(MV, "end")
                W.wait(MP, "A3_1")
                W.wait(MG, "end")
                for s in range(4):
                    e.wait_ge(spilled[s], e.snap((L * 12 + 13) * 16))
                LA.mark(e.activation(g2_hi[:], proj[:, 0:BT, :], ACT.Copy), "g2_hi")
                for q in range(4):
                    if q >= 2:
                        W.wait(LP, f"ssd_ss{q - 2}")
                    LA.mark(e.activation(ssq[:, q % 2, :], proj[:, Z + 2 * q:Z + 2 * q + 2, :].rearrange("p a b -> p (a b)"),
                                         ACT.Square), f"ssd_sq{q}")
                W.wait(LV, "ssd_v")
                LA.mark(e.activation(nrm[:, 1, :], nrm[:, 0, :], ACT.Sqrt), "ssd_sqrt")
                for q in range(4):
                    W.wait(LV, f"ssd_w{q}")
                    LA.mark(e.activation(ys[:, XS + 2 * q:XS + 2 * q + 2, :], proj[:, Z + 2 * q:Z + 2 * q + 2, :], ACT.Copy), f"ssd_hi{q}")
                nb = start(L, N_GLU)
                for j in range(4):
                    hi(nb, j + 2)
                    e.wait_ge(pair_done, nb[0] + (j + 3))
                    if j >= 2:
                        W.wait(LV, f"glu_a{j - 2}")
                    for a in range(2):
                        m = 2 * j + a
                        LA.mark(e.activation(tg[:, j % 2, a, :], mm[:, j % 2, a * 256:a * 256 + 256], ACT.Tanh, scale=0.25,
                                             bias=bgh[:, m:m + 1]), f"glu_t{m}")
                    W.wait(LV, f"glu_y{j}")
                    LA.mark(e.activation(ys[:, SG + 2 * j:SG + 2 * j + 2, :], proj[:, 2 * j:2 * j + 2, :], ACT.Copy), f"glu_hi{j}")
                W.wait(LV, "glu_lo3")
                with e.Fori(0, 2) as I:
                    nb = start(L, N_BR, I, 12)
                    g0 = e.snap(I * 24)
                    for j in range(12):
                        e.wait_ge(lo_done, nb[0] + (j + 1 + RAW))
                        W.settle()
                        e.dma_start(gin[:, j % 2], gscr.rearrange("(n a) p t -> n p a t", a=2)[I * 12 + j]).then_inc(gate_in[j % 2], 16)
                        hi(nb, j + 2)
                        for a in range(2):
                            u = 2 * j + a
                            if u % 3 == 2:
                                m = u // 3
                                e.wait_ge(merged, e.snap((L * 16 + I * 8 + (m + 1))))
                                W.settle()
                                e.activation(h_hi[:, bass.ds(I * 8 + m, 1), :], acc[:, m % 2, :], ACT.Copy).then_inc(merged_hi, 1)
                with e.Fori(0, 4) as I:
                    nb = start(L, N_OUT, I, 4)
                    for j in range(4):
                        hi(nb, j + 2)
                    e.wait_ge(lo_done, nb[0] + 6 + RAW)
                    e.dma_start(xs_out[L + 1][:, bass.ds(I * 4, 4), :], proj[:, bass.ds(I * 4, 4), :]).then_inc(x_out, 16)

        @block.vector
        def _(e):
            W = Where(e)
            e.sem_inc(LV.sem, 2 * LV.n)
            e.sem_inc(MV.sem, 2 * MV.n)
            e.sem_inc(lo_done, RAW)
            e.sem_inc(summed, 5)

            def lo(nb, j):
                e.wait_ge(hi_done, nb + (j + 1))
                e.tensor_tensor(w_lo[:, j % SPLIT, :], raw[:, j % RAW, :], w_hi[:, j % SPLIT, :].bitcast(F32),
                                ALU.subtract).then_inc(lo_done, 1)

            def tt_(out, a, b, op):
                return e.tensor_tensor(out, a, b, op)

            def newton(S, nm, y, t, v):
                W.wait(S, nm + "_r")
                S.mark(tt_(t, y, y, ALU.mult), nm + "_n1")
                W.wait(S, nm + "_n1")
                S.mark(tt_(t, t, v, ALU.mult), nm + "_n2")
                W.wait(S, nm + "_n2")
                S.mark(e.tensor_scalar(t, t, -0.5, 1.5, ALU.mult, ALU.add), nm + "_n3")
                W.wait(S, nm + "_n3")
                S.mark(tt_(y, y, t, ALU.mult), nm + "_n4")
                W.wait(S, nm + "_n4")

            lo(0, 0)
            lo(0, 1)
            with e.Fori(0, DEPTH) as L:
                W.layer(L)
                lw = e.snap(L * N_LAYER + RAW + 2)
                e.wait_ge(lo_done, lw)
                e.wait_ge(x_in, 16)
                e.wait_ge(const_in, 32)
                for k in range(KT):
                    ins = e.tensor_scalar(proj[:, 32 + k, :], proj[:, k, :], nw[:, bass.ds(L, 1), k:k + 1].rearrange("p a b -> p (a b)"),
                                          None, ALU.mult)
                    LV.mark(ins, f"xw{k // 4}" if k % 4 == 3 else f"xw_{k}")
                for q in range(4):
                    W.wait(LA, f"xhi{q}")
                    LV.mark(tt_(h_lo[:, 4 * q:4 * q + 4, :], proj[:, 32 + 4 * q:36 + 4 * q, :],
                                h_hi[:, 4 * q:4 * q + 4, :].bitcast(F32), ALU.subtract), f"xlo{q}")
                W.wait(LP, "ss")
                LV.mark(e.tensor_scalar(sv[:, 0, :], b4[:, 0:TOK], 1.0 / D_MODEL, EPS, ALU.mult, ALU.add), "rs_v")
                W.wait(LP, "sstok")
                LV.mark(e.tensor_scalar(small[:, 2:4], b5[:, 0:2], 1.0 / D_MODEL, EPS, ALU.mult, ALU.add), "rt_v")
                W.wait(LA, "rs_sqrt")
                LV.mark(e.reciprocal(rstd[:], sv[:, 1, :]), "rs_r")
                newton(LV, "rs", rstd[:], sv[:, 1, :], sv[:, 0, :])
                W.wait(LA, "rt_sqrt")
                LV.mark(e.reciprocal(rtok[:], small[:, 4:6]), "rt_r")
                newton(LV, "rt", rtok[:], small[:, 4:6], small[:, 2:4])

                count = [0]

                def chain(ins, name=None):
                    name = name or f"c{count[0]}"
                    count[0] += 1
                    LV.mark(ins, name)
                    W.wait(LV, name)

                def S(k):
                    return sp[:, k, :]
                a_re, a_im = PR("a_re", 0, ST), PR("a_im", 0, ST)
                e.wait_ge(par_in, e.snap((L + 1) * 16))
                W.wait(LA, "s5_dt")
                chain(tt_(S(1), a_re, S(0), ALU.mult), "s5_ax")
                chain(tt_(S(3), a_im, S(0), ALU.mult))
                chain(e.tensor_scalar(S(4), S(3), INV_2PI, ROUND, ALU.mult, ALU.add))
                chain(e.tensor_scalar(S(4), S(4), ROUND, None, ALU.subtract))
                for cpart in (C1, C2, C3):
                    chain(e.scalar_tensor_tensor(S(3), S(4), -cpart, S(3), ALU.mult, ALU.add))
                chain(e.tensor_scalar(S(3), S(3), INV_2PI, 0.5, ALU.mult, ALU.min))
                chain(e.tensor_scalar(S(3), S(3), -0.5, None, ALU.max))
                LV.mark(e.tensor_copy(s5p[:, 1, :], S(3)), "turns")
                LV.mark(e.tensor_copy(turn_hi[:], S(3)), "turn_hi")
                chain(e.scalar_tensor_tensor(S(4), S(3), -1.0, S(3), ALU.mult, ALU.max), "turn_abs")
                LV.mark(e.tensor_copy(s5p[:, 2, :], turn_hi[:].bitcast(F32)), "turn_hi2")
                LV.mark(tt_(s5p[:, 3, :], S(3), turn_hi[:].bitcast(F32), ALU.subtract), "turn_lo")
                W.wait(LA, "s5_tanh")
                chain(e.tensor_scalar(S(7), S(2), -1.0, 1.0, ALU.mult, ALU.add))
                chain(e.reciprocal(S(8), S(7)))
                chain(e.scalar_tensor_tensor(s5p[:, 0, :], S(2), 1.0, S(8), ALU.add, ALU.mult))
                chain(e.scalar_tensor_tensor(S(9), S(2), 2.0, S(8), ALU.mult, ALU.mult))
                W.wait(LA, "s5_cos")
                chain(tt_(S(6), S(5), S(6), ALU.mult))
                chain(tt_(S(5), S(5), S(5), ALU.mult))
                chain(tt_(S(5), S(5), s5p[:, 0, :], ALU.mult))
                chain(e.scalar_tensor_tensor(S(5), S(5), -2.0, S(9), ALU.mult, ALU.add))
                chain(e.scalar_tensor_tensor(S(6), S(6), 2.0, s5p[:, 0, :], ALU.mult, ALU.mult))
                chain(tt_(S(7), a_re, a_re, ALU.mult))
                chain(tt_(S(8), a_im, a_im, ALU.mult))
                chain(tt_(S(7), S(7), S(8), ALU.add))
                chain(e.reciprocal(S(8), S(7)))
                chain(tt_(S(9), S(5), a_re, ALU.mult))
                chain(tt_(S(10), S(6), a_im, ALU.mult))
                chain(tt_(S(9), S(9), S(10), ALU.add))
                chain(tt_(S(9), S(9), S(8), ALU.mult))
                chain(tt_(S(10), S(6), a_re, ALU.mult))
                chain(tt_(S(11), S(5), a_im, ALU.mult))
                chain(tt_(S(10), S(10), S(11), ALU.subtract))
                chain(tt_(S(10), S(10), S(8), ALU.mult))
                c_re = PR("c_re", 0, ST * 16).rearrange("p (j h) -> p j h", h=16)
                c_im = PR("c_im", 0, ST * 16).rearrange("p (j h) -> p j h", h=16)
                g_re = S(9).unsqueeze(2).broadcast_to([P, ST, 16])
                g_im = S(10).unsqueeze(2).broadcast_to([P, ST, 16])
                ca = cw[:, 0, :].rearrange("p (j h) -> p j h", h=16)
                cb = cw[:, 1, :].rearrange("p (j h) -> p j h", h=16)
                chain(tt_(ca, c_re, g_re, ALU.mult))
                chain(tt_(cb, c_im, g_im, ALU.mult))
                chain(tt_(ca, ca, cb, ALU.subtract))
                chain(tt_(cb, c_re, g_im, ALU.mult))
                chain(tt_(c_re, c_im, g_re, ALU.mult))
                chain(e.scalar_tensor_tensor(c_im, cb, -1.0, c_re, ALU.mult, ALU.subtract))
                chain(e.tensor_copy(c_re, ca))
                W.wait(LA, "wdt_hi")
                LV.mark(tt_(wdt_lo[:], PR("w_dt", 0, KT * 16).rearrange("p (k c) -> p k c", k=KT), wdt_hi[:].bitcast(F32),
                            ALU.subtract), "wdt_lo")

                nb = e.snap(L * N_LAYER)
                for j in range(8):
                    e.wait_ge(pair_done, nb + (j + 3))
                    if j < 4:
                        ins = tt_(proj[:, BC + j, :], mm[:, j % 2, 0:256], rstd[:], ALU.mult)
                    elif j < 6:
                        ins = tt_(kt[:, j - 4, :], mm[:, j % 2, 0:256], rstd[:], ALU.mult)
                    else:
                        for t in range(2):
                            ins = e.tensor_scalar(vt[:, t, (j - 6) * 128:(j - 5) * 128], mm[:, j % 2, t * 128:t * 128 + 128],
                                                  rtok[:, t:t + 1], None, ALU.mult)
                    lo(nb, j + 2)
                e.wait_ge(lo_done, nb + 10 + RAW)
                chain(e.tensor_scalar(small[:, 8:9], C("half_pi"), 0.0, None, ALU.mult), "k_raw")

                def D(k):
                    return sd[:, k, :]
                W.wait(LP, "dt")
                for t in range(2):
                    LV.mark(e.scalar_tensor_tensor(sd[:, 0, t * 16:t * 16 + 16], b6[:, t * 16:t * 16 + 16], rtok[:, t:t + 1],
                                                   PR("dt_bias", 0, 16), ALU.mult, ALU.add), f"dt_x{t}")
                W.wait(LV, "dt_x1")
                chain(e.scalar_tensor_tensor(D(1), D(0), -1.0, D(0), ALU.mult, ALU.max), "dt_abs")

                def conv(dst, src, wcol, S_, nm):
                    S_.mark(e.tensor_scalar(dst, src, wcol(3), wcol(4), ALU.mult, ALU.add), nm + "0")
                    for sft in range(1, 4):
                        W.wait(S_, nm + f"{sft - 1}")
                        S_.mark(e.scalar_tensor_tensor(dst[:, sft:TOK], src[:, 0:TOK - sft], wcol(3 - sft), dst[:, sft:TOK],
                                                       ALU.mult, ALU.add), nm + f"{sft}")

                for t in range(4):
                    dst = kk[:, 2, 0:TOK] if t % 2 == 0 else kk[:, 2, TOK:]
                    conv(dst, proj[:, BC + t, :], lambda k, t=t: PR("conv", (8 + t) * 5 + k), LV, f"bc_conv{t}_")
                    if t == 0:
                        W.wait(LA, "dt_exp")
                        chain(e.tensor_scalar(D(3), D(2), 2.0, None, ALU.add))
                        chain(e.reciprocal(D(4), D(3)))
                        chain(tt_(D(3), D(2), D(4), ALU.mult))
                        chain(tt_(D(4), D(3), D(3), ALU.mult))
                        chain(e.tensor_scalar(D(5), D(4), 1.0 / 17, None, ALU.mult))
                        for k in (15, 13, 11, 9, 7, 5, 3):
                            chain(e.scalar_tensor_tensor(D(5), D(5), 1.0 / k, D(4), ALU.add, ALU.mult))
                        chain(e.scalar_tensor_tensor(D(5), D(5), 1.0, D(3), ALU.add, ALU.mult))
                        chain(e.tensor_scalar(D(1), D(0), 0.0, None, ALU.max))
                        chain(e.scalar_tensor_tensor(D(7), D(5), 2.0, D(1), ALU.mult, ALU.add))
                        chain(e.tensor_scalar(dta[:, 1].rearrange("p a b -> p (a b)"), D(7), 0.5, None, ALU.mult))
                        chain(e.scalar_tensor_tensor(dta[:, 0], D(7).rearrange("p (a b) -> p a b", a=2), -1.0,
                                                     sd[:, 6, 0:16].unsqueeze(1).broadcast_to([P, 2, 16]), ALU.mult, ALU.mult))
                    W.wait(LA, f"bc_tanh{t}")
                    LV.mark(e.scalar_tensor_tensor(proj[:, BC + t, :], bt[:], 1.0, dst, ALU.add, ALU.mult), f"bc_silu{t}")
                for g in range(2):
                    W.wait(LP, f"G{g}")
                    b = (b4, b5)[g]
                    tri = C("tri", P)
                    LV.mark(e.scalar_tensor_tensor(gm[:, g, 0:128], b[:, 0:128], 0.25, tri, ALU.mult, ALU.mult), f"gm{g}0")
                    LV.mark(e.tensor_scalar(gm[:, g, 128:256], b[:, 128:256], 0.25, None, ALU.mult), f"gm{g}1")
                    LV.mark(e.scalar_tensor_tensor(gm[:, g, 256:384], b[:, 256:384], 0.25, tri, ALU.mult, ALU.mult), f"gm{g}2")
                W.wait(LP, "k_ss")
                LV.mark(e.tensor_scalar(kk[:, 3, :], b7[:], 1.0 / HD, EPS, ALU.mult, ALU.add), "k_v")
                W.wait(LA, "k_sqrt")
                LV.mark(e.reciprocal(kk[:, 0, :], kk[:, 1, :]), "k_r")
                newton(LV, "k", kk[:, 0, :], kk[:, 1, :], kk[:, 3, :])
                ktf = kt[:].rearrange("p a b -> p (a b)")
                chain(e.scalar_tensor_tensor(kk[:, 1, :], ktf, PR("k_norm"), kk[:, 0, :], ALU.mult, ALU.mult), "kn")

                def twice(a):
                    return a.unsqueeze(1).broadcast_to([P, 2, TOK])

                def two(a):
                    return a.rearrange("p (a b) -> p a b", a=2)
                LV.mark(tt_(two(kk[:, 0, :]), two(kk[:, 1, :]), twice(C("cos")), ALU.mult), "k_c")
                W.wait(LP, "k_rot")
                chain(tt_(two(kk[:, 3, :]), two(b6[:]), twice(C("sin")), ALU.mult))
                chain(tt_(ktf, kk[:, 0, :], kk[:, 3, :], ALU.add), "k_fin")
                chain(e.tensor_scalar(small[:, 9:10], C("half_pi"), 0.0, None, ALU.mult), "prep_end")

                e.wait_ge(x_out, e.snap((L + 1) * 64))
                W.settle()
                with e.Fori(0, 12) as I:
                    nb = e.snap(L * N_LAYER + N_IN + I * 4)
                    for j in range(4):
                        e.wait_ge(pair_done, nb + (j + 3))
                        tt_(proj[:, bass.ds(I * 4 + j, 1), :].rearrange("p a b -> p (a b)"), mm[:, j % 2, 0:256], rstd[:], ALU.mult)
                        lo(nb, j + 2)

                e.wait_ge(lo_done, e.snap(L * N_LAYER + N_GATE + 2 + RAW))
                W.settle()
                with e.Fori(0, 4) as I:
                    nb = e.snap(L * N_LAYER + N_GATE + I * 12)
                    sb0 = e.snap((L * 12 + I * 3 + 1) * 16)
                    for c in range(2):
                        W.tile(L, I, c)
                        i = I * 2 + c
                        cc = cur[:, c, :]

                        def slot(k):
                            return proj[:, bass.ds(i + k, 1), :].rearrange("p a b -> p (a b)")

                        def s5(j):
                            p1, p2 = prod[:, j % 2], prod2[:]
                            bu = b4[:].rearrange("p (a b) -> p a b", a=2)
                            cosb = tab[:, j % 2, 0, :].unsqueeze(1).broadcast_to([P, 2, TOK])
                            sinb = tab[:, j % 2, 1, :].unsqueeze(1).broadcast_to([P, 2, TOK])
                            W.wait(MP, f"bu{j}")
                            W.wait(MA, f"cos{j}")
                            W.wait(MP, f"C{j - 2}" if j >= 2 else f"C{j + 2}", 0 if j >= 2 else 1)
                            MV.mark(tt_(p1, bu, cosb, ALU.mult), f"p1_{j}")
                            W.wait(MV, f"sim{j - 1}" if j else "sim3", 0 if j else 1)
                            MV.mark(tt_(p2, bu, sinb, ALU.mult), f"p2_{j}")
                            W.wait(MV, f"p2_{j}")
                            MV.mark(tt_(p1[:, 0, :], p1[:, 0, :], p2[:, 1, :], ALU.add), f"vre{j}")
                            MV.mark(tt_(p1[:, 1, :], p1[:, 1, :], p2[:, 0, :], ALU.subtract), f"vim{j}")
                            dec = cc[:, j:j + 1].broadcast_to([P, TOK])
                            W.wait(MV, f"vre{j}")
                            MV.mark(e.tensor_tensor_scan(wst[:, 0, :], dec, p1[:, 0, :], 0.0, ALU.mult, ALU.add), f"wre{j}")
                            W.wait(MV, f"vim{j}")
                            MV.mark(e.tensor_tensor_scan(wst[:, 1, :], dec, p1[:, 1, :], 0.0, ALU.mult, ALU.add), f"wim{j}")
                            W.wait(MV, f"wim{j}")
                            MV.mark(tt_(p1, wst[:], cosb, ALU.mult), f"q1_{j}")
                            MV.mark(tt_(p2, wst[:], sinb, ALU.mult), f"q2_{j}")
                            W.wait(MV, f"q2_{j}")
                            MV.mark(tt_(p1[:, 0, :], p1[:, 0, :], p2[:, 1, :], ALU.subtract), f"sre{j}")
                            MV.mark(tt_(p1[:, 1, :], p1[:, 1, :], p2[:, 0, :], ALU.add), f"sim{j}")

                        def m1_make(h):
                            W.wait(MG, "cur1")
                            W.wait(MP, "diff0" if h else "diff1", 0 if h else 1)
                            for q, (nm, t) in enumerate((("strict", 0), ("ones", 1), ("strict", 1))):
                                MV.mark(e.tensor_scalar(m1[:, q, :], C(nm), cc[:, 16 + 2 * t + h:17 + 2 * t + h], None, ALU.mult),
                                        f"m1_{h}{q}")

                        def st_make(h):
                            W.wait(MA, f"ex{h}")
                            W.wait(MP, "ys0" if h else "ys1", 0 if h else 1)
                            MV.mark(tt_(stt_[:], ex[:], gm[:, bass.ds(I // 2, 1), :].rearrange("p a b -> p (a b)"), ALU.mult), f"ST{h}")

                        def att_scores(h):
                            W.wait(MP, f"A1_{h}")
                            W.wait(MA, "pes0" if h else "pes1", 0 if h else 1)
                            MV.mark(e.scalar_tensor_tensor(sc[:], b7[:, 0:384], HD ** -0.5, C("amask"), ALU.mult, ALU.add), f"sc{h}")
                            W.wait(MV, f"sc{h}")
                            W.wait(MV, f"den{h ^ 1}", 0 if h else 1)
                            MV.mark(e.tensor_reduce(small[:, 0:1], sc[:, 0:128], AX.X, ALU.max), f"mx0{h}")
                            MV.mark(e.tensor_reduce(small[:, 1:2], sc[:, 128:384], AX.X, ALU.max), f"mx1{h}")
                            W.wait(MV, f"mx1{h}")
                            MV.mark(e.tensor_scalar(small[:, 2:4], small[:, 0:2], cc[:, 24 + h:25 + h], -1.0, ALU.max, ALU.mult), f"nm{h}")

                        def att_norm(h):
                            W.wait(MA, f"pes{h}")
                            MV.mark(tt_(small[:, 6:8], small[:, 6:8], small[:, 4:6], ALU.add), f"den{h}")
                            W.wait(MV, f"den{h}")
                            MV.mark(e.reciprocal(small[:, 10:12], small[:, 6:8]), f"rden{h}")
                            W.wait(MV, f"rden{h}")
                            MV.mark(e.tensor_scalar(pr[:, 0:128], pr[:, 0:128], small[:, 10:11], None, ALU.mult), f"pn0{h}")
                            MV.mark(e.tensor_scalar(pr[:, 128:384], pr[:, 128:384], small[:, 11:12], None, ALU.mult), f"pn1{h}")

                        for t in range(6):
                            s = 6 * c + t
                            e.wait_ge(pair_done, nb + (s + 3))
                            e.wait_ge(spilled[s % 4], sb0 + 16 * (s // 4))
                            MV.mark(tt_(gt[:, s % 4, :], mm[:, s % 2, 0:256], rstd[:], ALU.mult), f"gt{t}")
                            lo(nb, s + 2)
                            if t == 0:
                                W.wait(MG, "cur5")
                                W.wait(MP, "xT", 1)
                                conv(xc[:], slot(XS), lambda k: cc[:, 28 + k:29 + k], MV, "conv")
                                W.wait(MA, "xc_tanh")
                                MV.mark(e.scalar_tensor_tensor(xc[:], tt[:], 1.0, xc[:], ALU.add, ALU.mult), "xc")
                                W.wait(MP, "q_ss")
                                MV.mark(e.tensor_scalar(rv[:], b7[:, 0:256], 1.0 / HD, EPS, ALU.mult, ALU.add), "q_v")
                                W.wait(MA, "q_sqrt")
                                MV.mark(e.reciprocal(qh[:], rq[:]), "q_r")
                                newton(MV, "q", qh[:], rq[:], rv[:])
                                MV.mark(e.scalar_tensor_tensor(qn[:], slot(Q), PR("q_norm"), qh[:], ALU.mult, ALU.mult), "qn")
                                s5(0)
                                W.wait(MV, "qn")
                                W.wait(MP, "A1_1", 1)
                                MV.mark(tt_(qh[:], qn[:], C("cos"), ALU.mult), "q_c")
                            if t == 1:
                                W.wait(MP, "xT")
                                W.wait(MP, "ys1", 1)
                                MV.mark(tt_(xdt[:], b6[:, 0:256].rearrange("p (a h d) -> p a h d", a=2, h=2),
                                            cc[:, 20:24].rearrange("p (a h) -> p a h", a=2).unsqueeze(3).broadcast_to([P, 2, 2, 64]),
                                            ALU.mult), "xdt")
                                W.wait(MP, "q_rot")
                                MV.mark(tt_(rq[:], b7[:, 256:512], C("sin"), ALU.mult), "q_s")
                                W.wait(MV, "q_s")
                                MV.mark(tt_(qh[:], qh[:], rq[:], ALU.add), "qh")
                                m1_make(0)
                                s5(1)
                            if t == 2:
                                att_scores(0)
                                s5(2)
                                st_make(0)
                                att_norm(0)
                                m1_make(1)
                            if t == 3:
                                att_scores(1)
                                s5(3)
                                st_make(1)
                                att_norm(1)
                            if t == 4:
                                W.wait(MP, "C3")
                                W.wait(MG, "cur3")
                                MV.mark(e.scalar_tensor_tensor(y5[:], slot(U), cc[:, 26:27], ps_s5, ALU.mult, ALU.add), "y5")
                                W.wait(MA, "tz")
                                MV.mark(e.scalar_tensor_tensor(qn[:], qn[:], 1.0, slot(Z), ALU.add, ALU.mult), "zb")
                                W.wait(MA, "ta")
                                MV.mark(e.scalar_tensor_tensor(rq[:], rq[:], 1.0, slot(AG), ALU.add, ALU.mult), "ab")
                                W.wait(MA, "ts")
                                MV.mark(e.scalar_tensor_tensor(slot(SG), rv[:], 1.0, slot(SG), ALU.add, ALU.mult), "sb")
                                W.wait(MA, "y5sq")
                                MV.mark(e.tensor_scalar(tt[:], tt[:], 0.044715, 1.0, ALU.mult, ALU.add), "g5a")
                                W.wait(MV, "g5a")
                                MV.mark(tt_(tt[:], tt[:], y5[:], ALU.mult), "g5b")
                                W.wait(MP, "ys1")
                                W.wait(MG, "cur4")
                                MV.mark(e.scalar_tensor_tensor(xc[:], xc[:], cc[:, 27:28], ps_ssd, ALU.mult, ALU.add), "yv")
                                W.wait(MV, "yv")
                                MV.mark(e.scalar_tensor_tensor(slot(Z), xc[:], 0.5, qn[:], ALU.mult, ALU.mult), "yz")
                            if t == 5:
                                W.wait(MA, "g5t")
                                MV.mark(e.scalar_tensor_tensor(slot(U), tt[:], 1.0, y5[:], ALU.add, ALU.mult), "s5g2")
                                W.wait(MP, "A3_1")
                                MV.mark(e.scalar_tensor_tensor(slot(Q), ps_att, 0.5, rq[:], ALU.mult, ALU.mult), "yatt")
                                W.wait(MA, "end")
                                MV.mark(tt_(ys[:, bass.ds(i + Q, 1), :].rearrange("p a b -> p (a b)"), slot(Q),
                                            ys[:, bass.ds(i + AG, 1), :].rearrange("p a b -> p (a b)").bitcast(F32), ALU.subtract), "end")

                W.last_tile(L)
                W.wait(MP, "A3_1")
                W.wait(MG, "end")
                W.wait(LA, "g2_hi")
                LV.mark(tt_(g2_lo[:], proj[:, 0:BT, :], g2_hi[:].bitcast(F32), ALU.subtract), "g2_lo")
                for s in range(4):
                    e.wait_ge(spilled[s], e.snap((L * 12 + 13) * 16))
                W.wait(LP, "ssd_ss3")
                LV.mark(e.tensor_scalar(nrm[:, 0, :], b4[:, 0:256], 1.0 / BW, EPS, ALU.mult, ALU.add), "ssd_v")
                W.wait(LA, "ssd_sqrt")
                LV.mark(e.reciprocal(acc[:, 0, :], nrm[:, 1, :]), "ssd_r")
                newton(LV, "ssd", acc[:, 0, :], nrm[:, 1, :], nrm[:, 0, :])
                for m in range(BT):
                    LV.mark(e.scalar_tensor_tensor(proj[:, Z + m, :], proj[:, Z + m, :], PR("ssd_norm", m), acc[:, 0, :],
                                                   ALU.mult, ALU.mult), f"ssd_w{m // 2}" if m % 2 else f"ssd_w_{m}")
                for q in range(4):
                    W.wait(LA, f"ssd_hi{q}")
                    LV.mark(tt_(ys[:, Z + 2 * q:Z + 2 * q + 2, :], proj[:, Z + 2 * q:Z + 2 * q + 2, :],
                                ys[:, XS + 2 * q:XS + 2 * q + 2, :].bitcast(F32), ALU.subtract), f"ssd_lo{q}")
                nb = e.snap(L * N_LAYER + N_GLU)
                for j in range(4):
                    W.wait(LA, f"glu_t{2 * j + 1}")
                    LV.mark(e.scalar_tensor_tensor(tg[:, j % 2], tg[:, j % 2], 1.0, proj[:, 2 * j:2 * j + 2, :], ALU.add, ALU.mult), f"glu_a{j}")
                    W.wait(LV, f"glu_a{j}")
                    LV.mark(e.scalar_tensor_tensor(proj[:, 2 * j:2 * j + 2, :], tg[:, j % 2], 0.125, proj[:, SG + 2 * j:SG + 2 * j + 2, :],
                                                   ALU.mult, ALU.mult), f"glu_y{j}")
                    W.wait(LA, f"glu_hi{j}")
                    LV.mark(tt_(ys[:, 2 * j:2 * j + 2, :], proj[:, 2 * j:2 * j + 2, :],
                                ys[:, SG + 2 * j:SG + 2 * j + 2, :].bitcast(F32), ALU.subtract), f"glu_lo{j}")
                    lo(nb, j + 2)

                W.settle()
                with e.Fori(0, 2) as I:
                    nb = e.snap(L * N_LAYER + N_BR + I * 12)
                    mb = e.snap(L * 16 + I * 8)
                    gb = e.snap((L * 12 + I * 6 + 1) * 16)
                    nsum = L * 80 + I * 40
                    sb_ = e.snap(nsum)
                    for j in range(12):
                        e.wait_ge(pair_done, nb + (j + 3))
                        e.wait_ge(gate_in[j % 2], gb + 16 * (j // 2))
                        for a in range(2):
                            u = 2 * j + a
                            m, b = u // 3, u % 3
                            k = 5 * m
                            dst = acc[:, m % 2, :] if b == 0 else tmp[:]
                            if b == 0:
                                e.wait_ge(merged_hi, mb + (m + 1))
                            else:
                                e.wait_ge(summed, sb_ + (k + (5, 8)[b - 1]))
                            ins = e.scalar_tensor_tensor(dst, gin[:, j % 2, a, :], 1.0, mm[:, j % 2, a * 256:a * 256 + 256], ALU.add, ALU.mult)
                            ins.then_inc(summed, 1)
                            if b:
                                e.wait_ge(summed, sb_ + (k + 2 * b + 5))
                                ins = tt_(acc[:, m % 2, :], acc[:, m % 2, :], tmp[:], ALU.add)
                                ins.then_inc(summed, 1)
                            if b == 2:
                                e.wait_ge(summed, sb_ + (k + 5 + 5))
                                e.tensor_scalar(acc[:, m % 2, :], acc[:, m % 2, :], 0.5, None, ALU.mult).then_inc(merged, 1)
                                e.wait_ge(merged_hi, mb + (m + 3))
                                tt_(h_lo[:, bass.ds(I * 8 + m, 1), :].rearrange("p a b -> p (a b)"), acc[:, m % 2, :],
                                    h_hi[:, bass.ds(I * 8 + m, 1), :].rearrange("p a b -> p (a b)").bitcast(F32), ALU.subtract).then_inc(merged_lo, 1)
                        lo(nb, j + 2)

                W.settle()
                with e.Fori(0, 4) as I:
                    nb = e.snap(L * N_LAYER + N_OUT + I * 4)
                    e.wait_ge(x_back, e.snap((L + 1) * 16))
                    for j in range(4):
                        e.wait_ge(pair_done, nb + (j + 3))
                        tt_(proj[:, bass.ds(I * 4 + j, 1), :].rearrange("p a b -> p (a b)"), mm[:, j % 2, 0:256],
                            proj[:, bass.ds(I * 4 + j + 16, 1), :].rearrange("p a b -> p (a b)"), ALU.add)
                        lo(nb, j + 2)

        @block.tensor
        def _(e):
            W = Where(e)
            e.sem_inc(LP.sem, 2 * LP.n)
            e.sem_inc(MP.sem, 2 * MP.n)
            e.sem_inc(pair_done, SPLIT)

            def prod3(out, whi, wlo, xhi, xlo, start, stop):
                e.matmul(out, whi, xlo, start=start, stop=False)
                e.matmul(out, wlo, xhi, start=False, stop=False)
                return e.matmul(out, whi, xhi, start=False, stop=stop)

            def pair(nb, j, xhi, xlo):
                e.wait_ge(lo_done, nb + (j + 1 + RAW))
                for k in range(KT):
                    w = slice(k * P, k * P + P)
                    ins = prod3(mm[:, j % 2, 0:256], w_hi[:, j % 2, w], w_lo[:, j % 2, w], xhi[:, k, :], xlo[:, k, :],
                                k == 0, k == KT - 1)
                ins.then_inc(pair_done, 1)

            def units(nb, j, sides):
                e.wait_ge(lo_done, nb + (j + 1 + RAW))
                for a in range(2):
                    xhi, xlo = sides[a]
                    for k in range(BT):
                        w = slice((a * BT + k) * P, (a * BT + k + 1) * P)
                        ins = prod3(mm[:, j % 2, a * 256:a * 256 + 256], w_hi[:, j % 2, w], w_lo[:, j % 2, w],
                                    xhi[:, k, :], xlo[:, k, :], k == 0, k == BT - 1)
                ins.then_inc(pair_done, 1)

            with e.Fori(0, DEPTH) as L:
                W.layer(L)
                for k in range(KT):
                    if k % 4 == 0:
                        W.wait(LA, f"xsq{k // 4}")
                    ins = e.matmul(b4[:, 0:TOK], C("ones"), proj[:, 16 + k, :], start=k == 0, stop=k == KT - 1)
                LP.mark(ins, "ss")
                for t in range(2):
                    for k in range(KT):
                        ins = e.matmul(b5[:, t:t + 1], proj[:, 16 + k, t * P:t * P + P], C("ones", 1), start=k == 0, stop=k == KT - 1)
                LP.mark(ins, "sstok")
                W.wait(LV, "xlo3")
                nb = e.snap(L * N_LAYER)
                for j in range(6):
                    pair(nb, j, h_hi, h_lo)
                for j in (6, 7):
                    e.wait_ge(lo_done, nb + (j + 1 + RAW))
                    for t in range(2):
                        for k in range(KT):
                            w, tok = slice(k * P, k * P + P), slice(t * P, t * P + P)
                            ins = prod3(mm[:, j % 2, tok], h_hi[:, k, tok], h_lo[:, k, tok], w_hi[:, j % 2, w], w_lo[:, j % 2, w],
                                        k == 0, k == KT - 1)
                    ins.then_inc(pair_done, 1)
                W.wait(LV, "wdt_lo")
                for t in range(2):
                    tok = slice(t * P, t * P + P)
                    for k in range(KT):
                        ins = prod3(b6[:, t * 16:t * 16 + 16], h_hi[:, k, tok], h_lo[:, k, tok], wdt_hi[:, k, :], wdt_lo[:, k, :],
                                    k == 0, k == KT - 1)
                LP.mark(ins, "dt")
                W.wait(LA, "k_sq")
                LP.mark(e.matmul(b7[:], C("blk"), kk[:, 0, :], start=True, stop=True), "k_ss")
                W.wait(LV, "bc_silu3")
                for g in range(2):
                    b = (b4, b5)[g]
                    e.matmul(b[:, 0:256], proj[:, BC + g, 0:P], proj[:, BC + 2 + g, :], start=True, stop=True)
                    LP.mark(e.matmul(b[:, 256:384], proj[:, BC + g, P:TOK], proj[:, BC + 2 + g, P:TOK], start=True, stop=True), f"G{g}")
                W.wait(LV, "kn")
                LP.mark(e.matmul(b6[:], C("rot"), kk[:, 1, :], start=True, stop=True), "k_rot")
                W.settle()
                with e.Fori(0, 12) as I:
                    nb = e.snap(L * N_LAYER + N_IN + I * 4)
                    for j in range(4):
                        pair(nb, j, h_hi, h_lo)

                W.settle()
                with e.Fori(0, 4) as I:
                    nb = e.snap(L * N_LAYER + N_GATE + I * 12)
                    for c in range(2):
                        W.tile(L, I, c)
                        i = I * 2 + c

                        def bu(j):
                            W.wait(MG, "bz1")
                            W.wait(MV, f"p2_{j - 1}" if j else "p2_3", 0 if j else 1)
                            for r in range(2):
                                ins = e.matmul(b4[:, r * 256:r * 256 + 256],
                                               bz[:, r, 2 * j:2 * j + 2, :].rearrange("p a b -> p (a b)"),
                                               proj[:, bass.ds(i + U, 1), :].rearrange("p a b -> p (a b)"), start=True, stop=True)
                            MP.mark(ins, f"bu{j}")

                        def cs(j):
                            if j == 0:
                                W.wait(MG, "cz11")
                                W.wait(MV, "y5", 1)
                            W.wait(MV, f"sim{j}")
                            for r in range(2):
                                ins = e.matmul(ps_s5[32 * j:32 * j + 32, :], cz[:, j, r, :], prod[:, j % 2, r, :],
                                               start=r == 0, stop=r == 1)
                            MP.mark(ins, f"C{j}")

                        def diff(h):
                            W.wait(MV, f"m1_{h}2")
                            W.wait(MA, f"ex{h ^ 1}", 0 if h else 1)
                            if not h:
                                W.wait(MV, "xdt")
                            e.matmul(b6[:, 0:256], m1[:, 0, :], C("tri"), start=True, stop=False)
                            e.matmul(b6[:, 128:256], m1[:, 1, :], C("tri", P), start=False, stop=True)
                            MP.mark(e.matmul(b6[:, 256:384], m1[:, 2, :], C("tri", P), start=True, stop=True), f"diff{h}")

                        def ssd_y(h):
                            W.wait(MV, f"ST{h}")
                            if not h:
                                W.wait(MV, "yatt", 1)
                            rows = slice(64 * h, 64 * h + 64)
                            e.matmul(ps_ssd[rows, :], xdt[:, 0, h, :], stt_[:, 0:256], start=True, stop=False)
                            MP.mark(e.matmul(ps_ssd[rows, 128:256], xdt[:, 1, h, :], stt_[:, 256:384], start=False, stop=True), f"ys{h}")

                        def a1(h):
                            W.wait(MV, f"sc{h ^ 1}", 0 if h else 1)
                            if not h:
                                W.wait(MV, "qh")
                                W.wait(MG, "vcur")
                                kv = e.snap((L * 4 + I + 1) * 32)
                                e.wait_ge(k_in, kv)
                            rows = slice(64 * h, 64 * h + 64)
                            e.matmul(b7[:, 0:128], qh[rows, 0:P], kcur[rows, 0:P], start=True, stop=True)
                            MP.mark(e.matmul(b7[:, 128:384], qh[rows, P:TOK], kcur[rows, :], start=True, stop=True), f"A1_{h}")

                        def a2(h):
                            W.wait(MV, f"pn1{h}")
                            W.wait(MA, f"pt{h ^ 1}", 0 if h else 1)
                            for q in range(3):
                                ins = e.transpose(b5[:, q * P:q * P + P], pr[:, q * P:q * P + P], C("ident"))
                            MP.mark(ins, f"A2_{h}")

                        def a3(h):
                            W.wait(MA, f"pt{h}")
                            W.wait(MV, "yv" if h else "yatt", 0 if h else 1)
                            rows = slice(64 * h, 64 * h + 64)
                            e.matmul(ps_att[rows, :], vcur[:, 0, :], pt[:, 0:256], start=True, stop=False)
                            MP.mark(e.matmul(ps_att[rows, 128:256], vcur[:, 1, :], pt[:, 256:384], start=False, stop=True), f"A3_{h}")

                        for t in range(6):
                            pair(nb, 6 * c + t, h_hi, h_lo)
                            if t == 0:
                                W.wait(MA, "q_sq")
                                W.wait(MV, "q_s", 1)
                                W.wait(MV, "sc1", 1)
                                MP.mark(e.matmul(b7[:, 0:256], C("blk"), tt[:], start=True, stop=True), "q_ss")
                                bu(0)
                            if t == 1:
                                W.wait(MV, "xc")
                                W.wait(MA, "ex1", 1)
                                for a in range(2):
                                    ins = e.transpose(b6[:, a * P:a * P + P], xc[:, a * P:a * P + P], C("ident"))
                                MP.mark(ins, "xT")
                                W.wait(MV, "qn")
                                MP.mark(e.matmul(b7[:, 256:512], C("rot"), qn[:], start=True, stop=True), "q_rot")
                                cs(0)
                                bu(1)
                            if t == 2:
                                a1(0)
                                cs(1)
                                bu(2)
                                diff(0)
                            if t == 3:
                                a2(0)
                                a1(1)
                                cs(2)
                                bu(3)
                                ssd_y(0)
                                diff(1)
                            if t == 4:
                                cs(3)
                                a3(0)
                                a2(1)
                                ssd_y(1)
                            if t == 5:
                                a3(1)

                W.last_tile(L)
                for q in range(4):
                    W.wait(LA, f"ssd_sq{q}")
                    for a in range(2):
                        ins = e.matmul(b4[:, 0:256], C("ones"), ssq[:, q % 2, a * 256:a * 256 + 256],
                                       start=(q == 0 and a == 0), stop=(q == 3 and a == 1))
                    LP.mark(ins, f"ssd_ss{q}")
                W.wait(LV, "g2_lo")
                nb = e.snap(L * N_LAYER + N_GLU)
                for j in range(4):
                    units(nb, j, [(g2_hi, g2_lo)] * 2)
                sides = [(ys[:, SG:SG + BT, :], ys[:, U:U + BT, :]), (ys[:, XS:XS + BT, :], ys[:, Z:Z + BT, :]),
                         (ys[:, AG:AG + BT, :], ys[:, Q:Q + BT, :])]
                W.wait(LV, "glu_lo3")
                W.settle()
                with e.Fori(0, 2) as I:
                    nb = e.snap(L * N_LAYER + N_BR + I * 12)
                    for j in range(12):
                        units(nb, j, [sides[(2 * j + a) % 3] for a in range(2)])
                e.wait_ge(merged_lo, e.snap((L + 1) * KT))
                W.settle()
                with e.Fori(0, 4) as I:
                    nb = e.snap(L * N_LAYER + N_OUT + I * 4)
                    for j in range(4):
                        pair(nb, j, h_hi, h_lo)

        found = {}
        for k, s in steps.items():
            n = len(s.seen) // (2 if k[0] == "M" else 1)
            assert s.seen == s.seen[:n] * (2 if k[0] == "M" else 1) and len(set(s.seen[:n])) == n, k
            assert order is None or s.names == s.seen[:n]
            found[k] = s.seen[:n]
        return found


INPUTS = ("x", "norm_w", "params", "consts", "bdense", "stream")


def lay_out(i):
    f = np.float32

    def tiles(a, n):
        return a.reshape(DEPTH, n, P).transpose(0, 2, 1)

    def states(a):
        return a.reshape(DEPTH, ST, 2, S5_STATE).transpose(0, 2, 3, 1).reshape(DEPTH, P, ST)

    def rows(a):
        return np.broadcast_to(a[:, None, :], (DEPTH, P, a.shape[1]))

    w_in = i["w_in"].reshape(DEPTH, KT, P, -1)
    at = {}
    o = 0
    for n, w in (("u", BW), ("sg", BW), ("z", BW), ("xs", BW), ("bc", 512), ("dt", 16), ("q", BW), ("k", 256), ("v", 256),
                 ("ag", BW), ("gates", 3 * D_MODEL)):
        at[n] = o
        o += w
    par = {
        "a_re": states(i["s5_a_re"]), "a_im": states(i["s5_a_im"]),
        "log_dt": states(np.broadcast_to(i["s5_log_dt"][:, :, None], (DEPTH, S5_GROUPS, S5_STATE))),
        "s5_d": tiles(i["s5_d"], BT), "b_glu": tiles(i["s5_b_glu"], BT),
        "conv": np.concatenate([i["ssd_conv_w"], i["ssd_conv_b"][:, None]], 1).reshape(DEPTH, 5, 12, P).transpose(0, 3, 2, 1)
        .reshape(DEPTH, P, 60),
        "ssd_norm": tiles(i["ssd_norm_w"], BT),
        "ssd_d": tiles(np.repeat(i["ssd_d"], HD, axis=1), BT),
        "q_norm": np.tile(i["att_q_norm"], (1, 2))[:, :, None], "k_norm": np.tile(i["att_k_norm"], (1, 2))[:, :, None],
        "dt_bias": rows(i["ssd_dt_bias"]), "a_log": rows(i["ssd_a_log"]), "sinks": rows(i["att_sinks"]),
        "w_dt": w_in[:, :, :, at["dt"]:at["dt"] + 16].transpose(0, 2, 1, 3).reshape(DEPTH, P, KT * 16),
        "c_re": i["s5_c_re"].reshape(DEPTH, ST, 2, 16, 64).transpose(0, 2, 4, 1, 3).reshape(DEPTH, P, ST * 16),
        "c_im": i["s5_c_im"].reshape(DEPTH, ST, 2, 16, 64).transpose(0, 2, 4, 1, 3).reshape(DEPTH, P, ST * 16),
    }
    params = np.empty((DEPTH, P, NPP), f)
    for n, (a, w) in PP.items():
        params[:, :, a:a + w] = par[n]
    b = np.stack([i["s5_b_re"], i["s5_b_im"]], 3)
    bdense = b.reshape(DEPTH, BT, 8, S5_STATE, 2, S5_GROUP).transpose(0, 1, 2, 5, 4, 3).reshape(DEPTH, BT, P, 2 * S5_STATE)

    stream = np.empty((DEPTH, N_LAYER, P, PAIR), f)

    def full(n, w4, col):
        stream[:, n] = w4[:, :, :, col:col + P].transpose(0, 2, 1, 3).reshape(DEPTH, P, PAIR)

    def unit(n, a, w4, col):
        stream[:, n, :, a * 1024:a * 1024 + 1024] = w4[:, :, :, col:col + P].transpose(0, 2, 1, 3).reshape(DEPTH, P, 1024)

    for m in range(4):
        full(N_BC + m, w_in, at["bc"] + m * P)
    for m in range(2):
        full(N_KV + m, w_in, at["k"] + m * P)
        full(N_KV + 2 + m, w_in, at["v"] + m * P)
    for s, n in ((U, "u"), (SG, "sg"), (Z, "z"), (XS, "xs"), (Q, "q"), (AG, "ag")):
        for m in range(BT):
            full(N_IN + s + m, w_in, at[n] + m * P)
    for m in range(KT):
        for br in range(3):
            full(N_GATE + 3 * m + br, w_in, at["gates"] + br * D_MODEL + m * P)
    glu = i["s5_w_glu"].reshape(DEPTH, BT, P, BW)
    for m in range(BT):
        unit(N_GLU + m // 2, m % 2, glu, m * P)
    for m in range(KT):
        for br in range(3):
            u = 3 * m + br
            unit(N_BR + u // 2, u % 2, i["w_branch"][:, br].reshape(DEPTH, BT, P, D_MODEL), m * P)
    w_out = i["w_out"].reshape(DEPTH, KT, P, D_MODEL)
    for m in range(KT):
        full(N_OUT + m, w_out, m * P)
    return {
        "x": np.ascontiguousarray(i["x"][0].T.reshape(KT, P, TOK).transpose(1, 0, 2)),
        "norm_w": np.ascontiguousarray(i["norm_w"].reshape(DEPTH, KT, P).transpose(2, 0, 1)),
        "params": params, "consts": constants(), "bdense": np.ascontiguousarray(bdense),
        "stream": stream.reshape(DEPTH * N_LAYER, P, PAIR),
    }


def declare(nc, arrays):
    args = [nc.dram_tensor(f"in_{n}", arrays[n].shape, F32, kind="ExternalInput").ap() for n in INPUTS]
    return args + [nc.dram_tensor("out_0", (DEPTH + 1, P, KT, TOK), F32, kind="ExternalOutput").ap()]


def kernel(**inputs):
    import concourse.bacc as _bacc
    from concourse.bass_utils import run_bass_kernel_spmd as _run

    arrays = lay_out({k: np.asarray(v) for k, v in inputs.items()})
    order = None
    for _ in range(2):
        nc = _bacc.Bacc("TRN2", target_bir_lowering=False, num_devices=1)
        order = program(nc, *declare(nc, arrays), order)
    r = _run(nc, [{f"in_{n}": arrays[n] for n in INPUTS}], core_ids=[0])
    y = r.results[0]["out_0"][DEPTH]
    return np.ascontiguousarray(y.transpose(1, 0, 2).reshape(D_MODEL, TOK).T)[None]
```

```python
import math
from contextlib import ExitStack

import numpy as np

import concourse.bass as bass
from concourse import mybir

F32 = mybir.dt.float32
F32R = mybir.dt.float32r
ALU = mybir.AluOpType
ACT = mybir.ActivationFunctionType
AX = mybir.AxisListType

P = 128
D_MODEL, TOK, DEPTH = 2048, 256, 2
KT = D_MODEL // P
BW = D_MODEL // 2
BT = BW // P
S5_GROUPS, S5_GROUP, S5_STATE = 64, 16, 64
ST = S5_GROUPS * S5_STATE // P
HEADS, KV_HEADS, HD = 16, 4, 64
CONV = 4
EPS = 1e-6

PAIR = 2048
RAW, SPLIT = 2, 2
N_BC, N_KV, N_U, N_IN, N_GATE = 0, 4, 8, 16, 48
N_SG, N_GLU, N_BR, N_OUT, N_LAYER = 96, 104, 108, 132, 148
BRANCHES = (1, 2, 0)

U, SG, Z, XS, Q, AG, BC = 0, 8, 16, 24, 32, 40, 48
NSLOT = 52

PP = {}
_at = 0
for _n, _w in (("a_re", ST), ("a_im", ST), ("log_dt", ST), ("s5_d", BT), ("b_glu", BT), ("conv", 12 * 5),
               ("ssd_norm", BT), ("ssd_d", BT), ("q_norm", 1), ("k_norm", 1), ("dt_bias", 16), ("a_log", 16),
               ("sinks", 16), ("w_dt", KT * 16), ("c_re", ST * 16), ("c_im", ST * 16)):
    PP[_n] = (_at, _w)
    _at += _w
NPP = _at

CC = {}
_at = 0
for _n, _w in (("tri", TOK), ("strict", P), ("ident", P), ("ones", P), ("blk", P), ("rot", P), ("amask", 384),
               ("cos", TOK), ("sin", TOK), ("iota", TOK), ("bmask", 8), ("half_pi", 1), ("eps", 1)):
    CC[_n] = (_at, _w)
    _at += _w
NCC = _at

TWO_PI = 6.2831850
INV_2PI = 1.0 / (2.0 * math.pi)
C1 = 6.28125
C2 = 0.0019340515136718750
C3 = 2.0 * math.pi - C1 - C2
ROUND = 12582912.0
GELU = math.sqrt(2.0 / math.pi)


def constants():
    c = np.zeros((P, NCC), np.float32)
    k = np.arange(P)

    def put(name, a):
        at, w = CC[name]
        c[:, at:at + w] = np.asarray(a, np.float32).reshape(P, w)

    put("tri", np.concatenate([(k[:, None] <= k[None, :]), np.ones((P, P))], 1))
    put("strict", k[:, None] > k[None, :])
    put("ident", np.eye(P))
    put("ones", np.ones((P, P)))
    put("blk", (k[:, None] // HD) == (k[None, :] // HD))
    rot = np.zeros((P, P))
    half = HD // 8
    for h in (0, HD):
        for i in range(half):
            rot[h + half + i, h + i] = -1.0
            rot[h + i, h + half + i] = 1.0
    put("rot", rot)
    q = k // 64
    m = np.full((P, 384), -1e30)
    key0 = np.arange(128) // 64
    m[:, :128][(key0[None, :] <= q[:, None]) & (key0[None, :] >= q[:, None] - 1)] = 0.0
    key1 = np.arange(256) // 64
    m[:, 128:][(key1[None, :] <= q[:, None] + 2) & (key1[None, :] >= q[:, None] + 1)] = 0.0
    put("amask", m)
    inv = (np.float32(500000.0) ** (-np.arange(half, dtype=np.float32) * np.float32(2.0) / np.float32(HD // 4))).astype(np.float32)
    ang = (np.arange(TOK, dtype=np.float32)[:, None] * inv[None, :]).astype(np.float32).astype(np.float64)
    cos, sin = np.ones((P, TOK)), np.zeros((P, TOK))
    for h in (0, HD):
        for i in range(half):
            for r in (h + i, h + half + i):
                cos[r], sin[r] = np.cos(ang[:, i]), np.sin(ang[:, i])
    put("cos", cos)
    put("sin", sin)
    put("iota", np.broadcast_to(np.arange(TOK), (P, TOK)))
    put("bmask", (k[:, None] // S5_GROUP) == np.arange(8)[None, :])
    put("half_pi", np.full((P, 1), math.pi / 2))
    put("eps", np.full((P, 1), EPS))
    return c


class Steps:

    def __init__(self, sem, names):
        self.sem, self.names, self.seen = sem, names, []

    def mark(self, ins, name):
        self.seen.append(name)
        ins.then_inc(self.sem, 1)
        return ins

    @property
    def n(self):
        return len(self.names) if self.names else 1

    def place(self, name):
        return self.names.index(name) + 1 if self.names else 1


def program(nc, x, norm_w, params, consts, bdense, stream, xs_out, order):
    with ExitStack() as ctx:
        def sem(name):
            return ctx.enter_context(nc.semaphore(name))

        base = (nc.sbuf_base + 31) // 32 * 32
        top = [base]

        def at(name, shape, dt, offset):
            return nc.alloc_sbuf_tensor_at(name, shape, dt, offset=offset)

        def sb(name, shape, dt=F32):
            n = 4
            for d in shape[1:]:
                n *= d
            o = top[0]
            top[0] += (n + 31) // 32 * 32
            return at(name, shape, dt, o)

        raw = sb("raw", [P, RAW, PAIR])
        w_hi = sb("w_hi", [P, SPLIT, PAIR], F32R)
        w_lo = sb("w_lo", [P, SPLIT, PAIR], F32R)
        h_hi = sb("h_hi", [P, KT, TOK], F32R)
        h_lo = sb("h_lo", [P, KT, TOK], F32R)
        o_proj = top[0]
        proj = sb("proj", [P, NSLOT, TOK])
        ys = at("ys", [P, NSLOT, TOK], F32R, o_proj)
        cst = sb("cst", [P, NCC])
        par = sb("par", [P, NPP])
        nw = sb("nw", [P, DEPTH + 1, KT])
        kt = sb("kt", [P, 2, TOK])
        vt = sb("vt", [P, 2, TOK])
        rstd = sb("rstd", [P, TOK])
        ssum = sb("ssum", [P, TOK])
        rtok = sb("rtok", [P, 2])
        gm = sb("gm", [P, 2, 384])
        s5p = sb("s5p", [P, 4, ST])
        turn_hi = sb("turn_hi", [P, ST], F32R)
        dta = sb("dta", [P, 2, 2, 16])
        bgh = sb("bgh", [P, BT])
        work = top[0]
        tab = sb("tab", [P, 2, 2, TOK])
        prod = sb("prod", [P, 2, 2, TOK])
        prod2 = sb("prod2", [P, 2, TOK])
        wst = sb("wst", [P, 2, TOK])
        frac = sb("frac", [P, 2, TOK])
        tA = sb("tA", [P, TOK])
        tB = sb("tB", [P, TOK])
        zabs = sb("zabs", [P, TOK])
        bz = sb("bz", [P, 2, 8, 64])
        cz = sb("cz", [P, 4, 2, 32])
        bd = sb("bd", [P, 2 * 64])
        cur = sb("cur", [P, 2, 32])
        cur5 = sb("cur5", [P, 20])
        xc = sb("xc", [P, TOK])
        tt = sb("tt", [P, TOK])
        xdt = sb("xdt", [P, 2, 2, 64])
        m1 = sb("m1", [P, 3, P])
        ex = sb("ex", [P, 384])
        stt_ = sb("stt", [P, 384])
        sc = sb("sc", [P, 384])
        pr = sb("pr", [P, 384])
        pt = sb("pt", [P, 2, 384])
        qn = sb("qn", [P, TOK])
        qh = sb("qh", [P, TOK])
        rq = sb("rq", [P, TOK])
        rv = sb("rv", [P, TOK])
        y5 = sb("y5", [P, TOK])
        t5 = sb("t5", [P, TOK])
        tq = sb("tq", [P, TOK])
        tz = sb("tz", [P, TOK])
        ta = sb("ta", [P, TOK])
        kcur = sb("kcur", [P, TOK])
        vcur = sb("vcur", [P, 2, 64])
        small = sb("small", [P, 16])
        gt = sb("gt", [P, 4, TOK])
        end = top[0]
        w0 = [work]

        def al(name, shape, dt=F32):
            n = 4
            for d in shape[1:]:
                n *= d
            o = w0[0]
            w0[0] += (n + 31) // 32 * 32
            assert w0[0] <= end
            return at(name, shape, dt, o)

        sp = al("sp", [P, 12, ST])
        cw = al("cw", [P, 2, ST * 16])
        wdt_hi = al("wdt_hi", [P, KT, 16], F32R)
        wdt_lo = al("wdt_lo", [P, KT, 16], F32R)
        sd = al("sd", [P, 8, 32])
        kk = al("kk", [P, 4, 2 * TOK])
        bt = al("bt", [P, TOK])
        sv = al("sv", [P, 2, TOK])
        w0[0] = work
        x_old = al("x_old", [P, KT, TOK])
        w0[0] = work
        g2_hi = al("g2_hi", [P, BT, TOK], F32R)
        g2_lo = al("g2_lo", [P, BT, TOK], F32R)
        nrm = al("nrm", [P, 2, TOK])
        ssq = al("ssq", [P, 2, 2 * TOK])
        tg = al("tg", [P, 2, 2, TOK])
        tsg = al("tsg", [P, 2, 2, TOK])
        gin = al("gin", [P, 2, 2, TOK])
        acc = al("acc", [P, 2, TOK])
        tmp = al("tmp", [P, TOK])
        assert end <= nc.sbuf_usable_end

        mm = ctx.enter_context(nc.psum_tensor("mm", [P, 2, 512], F32))
        bs = ctx.enter_context(nc.psum_tensor("bs", [P, 512], F32))
        by = ctx.enter_context(nc.psum_tensor("by", [P, 512], F32))
        b4 = ctx.enter_context(nc.psum_tensor("b4", [P, 512], F32))
        b5 = ctx.enter_context(nc.psum_tensor("b5", [P, 512], F32))
        b6 = ctx.enter_context(nc.psum_tensor("b6", [P, 512], F32))
        b7 = ctx.enter_context(nc.psum_tensor("b7", [P, 512], F32))
        ps_s5 = bs[:, 0:256]
        ps_ssd = by[:, 0:256]
        ps_att = by[:, 256:512]

        gscr = nc.dram_tensor("gscr", [3 * KT, P, TOK], F32)
        kscr = nc.dram_tensor("kscr", [2, P, TOK], F32)

        landed = [sem(f"landed{i}") for i in range(RAW)]
        hi_done = sem("hi_done")
        lo_done = sem("lo_done")
        pair_done = sem("pair_done")
        spilled = [sem(f"spilled{i}") for i in range(4)]
        const_in = sem("const_in")
        x_in = [sem(f"x_in{q}") for q in range(4)]
        nw_in = sem("nw_in")
        nw_pad = sem("nw_pad")
        x_copied = sem("x_copied")
        par_in = sem("par_in")
        k_out = sem("k_out")
        k_in = sem("k_in")
        b_in = sem("b_in")
        gate_in = [sem(f"gate_in{i}") for i in range(2)]
        x_back = sem("x_back")
        x_new = sem("x_new")
        x_w = sem("x_w")
        x_sq = sem("x_sq")
        x_sum = sem("x_sum")
        x_out = sem("x_out")
        passed = sem("passed")
        merged = sem("merged")
        merged_hi = sem("merged_hi")
        merged_lo = sem("merged_lo")
        summed = sem("summed")

        steps = {}
        for kind in ("L", "M", "S"):
            for e in "PVAG":
                s = Steps(sem({"P": "pe", "V": "vec", "A": "act", "G": "pool"}[e] + {"L": "_layer", "M": "_mix", "S": "_s5"}[kind]),
                          None if order is None else order[kind + e])
                steps[kind + e] = s
        LP, LV, LA, LG = (steps["L" + e] for e in "PVAG")
        MP, MV, MA, MG = (steps["M" + e] for e in "PVAG")
        SP, SV, SA, SGp = (steps["S" + e] for e in "PVAG")

        def C(name, w=None):
            a, n = CC[name]
            return cst[:, a:a + (w or n)]

        def PR(name, a=0, n=1):
            o = PP[name][0] + a
            return par[:, o:o + n]

        class Where:

            def __init__(self, e):
                self.e, self.b = e, {}

            def layer(self, L):
                for s in (LP, LV, LA, LG):
                    self.b[s] = self.e.snap((L + 2) * s.n)

            def tile(self, L, I, c):
                for s in (MP, MV, MA, MG):
                    self.b[s] = self.e.snap((L * 8 + I * 2 + (c + 2)) * s.n)

            def s5(self, L, I, more):
                for s in (SP, SV, SA, SGp):
                    self.b[s] = self.e.snap((L * 8 + I + (more + 2)) * s.n)

            def last_tile(self, L):
                for s in (MP, MV, MA, MG, SP, SV, SA, SGp):
                    self.b[s] = self.e.snap((L * 8 + 9) * s.n)

            def wait(self, s, name, back=0):
                self.e.wait_ge(s.sem, self.b[s] + (s.place(name) - back * s.n))

            def settle(self):
                self.e.sem_inc(passed, 1)

        block = ctx.enter_context(nc.Block())

        @block.sync
        def _(e):
            for q in range(4):
                e.dma_start(proj[:, 4 * q:4 * q + 4, :], x[:, 4 * q:4 * q + 4, :]).then_inc(x_in[q], 16)
                if q == 0:
                    e.dma_start(nw[:, 0:DEPTH, :], norm_w).then_inc(nw_in, 16)
            for j in range(RAW):
                e.dma_start(raw[:, j, :], stream[j]).then_inc(landed[j], 16)
            e.dma_start(cst[:], consts).then_inc(const_in, 16)
            e.dma_start(xs_out[0], x).then_inc(x_copied, 16)
            W = Where(e)

            def load(nb, j):
                e.wait_ge(lo_done, nb + (j + 1 + RAW))
                e.dma_start(raw[:, j % RAW, :], stream[nb + (j + RAW)]).then_inc(landed[j % RAW], 16)

            with e.Fori(0, DEPTH) as L:
                with e.Fori(0, N_GATE // 2 + 1) as I:
                    nb = e.snap(L * N_LAYER + I * 2)
                    for j in range(2):
                        load(nb, j)
                with e.Fori(0, 4) as I:
                    nb = e.snap(L * N_LAYER + N_GATE + I * 12)
                    g0 = e.snap(I * 12)
                    for c in range(2):
                        W.b[MA] = e.snap((L * 8 + I * 2 + (c + 2)) * MA.n)
                        for t in range(6):
                            s = 6 * c + t
                            W.wait(MA, f"gate{t}")
                            e.dma_start(gscr[g0 + s], gt[:, s % 4, :]).then_inc(spilled[s % 4], 16)
                            load(nb, s + 2)
                with e.Fori(0, (N_BR - N_SG) // 2 - 1) as I:
                    nb = e.snap(L * N_LAYER + (N_SG + 2) + I * 2)
                    for j in range(2):
                        load(nb, j)
                for s in range(4):
                    e.wait_ge(spilled[s], e.snap((L * 12 + 13) * 16))
                W.settle()
                with e.Fori(0, (N_OUT - N_BR) // 2) as I:
                    nb = e.snap(L * N_LAYER + N_BR + I * 2)
                    for j in range(2):
                        load(nb, j)
                        e.dma_start(gin[:, j % 2], gscr.rearrange("(n a) p t -> n p a t", a=2)[I * 2 + j]).then_inc(gate_in[j % 2], 16)
                with e.Fori(0, (N_LAYER - N_OUT) // 2) as I:
                    nb = e.snap(L * N_LAYER + N_OUT + I * 2)
                    for j in range(2):
                        load(nb, j)
            e.wait_ge(x_out, (DEPTH + 1) * 64)
            e.wait_ge(x_copied, 16)

        @block.gpsimd
        def _(e):
            W = Where(e)
            for s in (LG, MG, SGp):
                e.sem_inc(s.sem, 2 * s.n)
            e.sem_inc(x_out, 64)
            e.sem_inc(x_sum, 1)

            def sum_squares(first, tile, known):
                e.wait_ge(x_sq, first)
                e.wait_ge(x_sum, first)
                W.settle()
                e.tensor_tensor(ssum[:], ssum[:], tile, ALU.add).then_inc(x_sum, 1)

            e.memset(nw[:, DEPTH, :], 1.0).then_inc(nw_pad, 1)
            e.memset(ssum[:], 0.0).then_inc(x_sum, 1)
            for m in range(KT):
                e.wait_ge(x_sq, m + 1)
                e.wait_ge(x_sum, m + 2)
                e.tensor_tensor(ssum[:], ssum[:], proj[:, 16 + m, :], ALU.add).then_inc(x_sum, 1)

            def s5_tile(L, I, more, between):
                W.s5(L, I, more)
                i = I + more
                W.wait(SGp, "end", 1)
                SGp.mark(e.tensor_copy(cur5[:, 0:12].rearrange("p (a b) -> p a b", a=3),
                                       s5p[:, 1:4, bass.ds(I * 4 + more * 4, 4)]), "cur")
                e.dma_start(bd[:], bdense[L, i]).then_inc(b_in, 16)

                def turns(j):
                    if j < 2:
                        W.wait(SA, f"cos{j + 2}", 1)
                    else:
                        W.wait(SA, f"cos{j - 2}")
                    W.wait(SGp, ("cur", "frac0", "d", "frac2")[j])
                    if j == 2 and more:
                        W.wait(MG, "end")
                    W.settle()
                    SGp.mark(e.tensor_scalar(tA[:], C("iota"), cur5[:, j:1 + j], ROUND, ALU.mult, ALU.add), f"ta{j}")
                    SGp.mark(e.tensor_scalar(tB[:], C("iota"), cur5[:, 4 + j:5 + j], 0.0, ALU.mult, ALU.add), f"tb{j}")
                    W.wait(SGp, f"ta{j}")
                    W.settle()
                    SGp.mark(e.tensor_scalar(tA[:], tA[:], -ROUND, 1.0, ALU.add, ALU.mult), f"tc{j}")
                    W.wait(SGp, f"tc{j}")
                    SGp.mark(e.tensor_tensor(tB[:], tB[:], tA[:], ALU.subtract), f"td{j}")
                    W.wait(SGp, f"td{j}")
                    W.settle()
                    SGp.mark(e.tensor_scalar(tA[:], C("iota"), cur5[:, 8 + j:9 + j], 0.0, ALU.mult, ALU.add), f"te{j}")
                    W.wait(SGp, f"te{j}")
                    SGp.mark(e.tensor_tensor(tB[:], tB[:], tA[:], ALU.add), f"tf{j}")
                    W.wait(SGp, f"tf{j}")
                    W.settle()
                    SGp.mark(e.tensor_scalar(frac[:, j % 2, :], tB[:], 0.5, -0.5, ALU.min, ALU.max), f"frac{j}")

                turns(0)
                turns(1)
                W.wait(SGp, "frac1")
                e.wait_ge(b_in, e.snap((L * 8 + i + 1) * 16))
                W.wait(SP, "bu3", 1)
                for r in range(2):
                    SGp.mark(e.tensor_tensor(bz[:, r], bd[:, r * 64:r * 64 + 64].unsqueeze(1).broadcast_to([P, 8, 64]),
                                             C("bmask").unsqueeze(2).broadcast_to([P, 8, 64]), ALU.mult), f"bz{r}")
                W.wait(SP, "C3", 1)
                for g in range(2):
                    rows = slice(64 * g, 64 * g + 64)
                    for r, nm in enumerate(("c_re", "c_im")):
                        W.wait(SGp, "bz1" if (g, r) == (0, 0) else f"cz{g}0" if r else "cz01")
                        SGp.mark(e.tensor_copy(cz[rows, :, r, 16 * g:16 * g + 16],
                                               par[rows, bass.ds(i * 64 + PP[nm][0], 64)].rearrange("p (j h) -> p j h", j=4)),
                                 f"cz{g}{r}")
                W.wait(SV, "y5", 1)
                W.wait(SGp, "cz11")
                W.settle()
                SGp.mark(e.tensor_copy(cur5[:, 12:16], s5p[:, 0, bass.ds(I * 4 + more * 4, 4)]), "decay")
                SGp.mark(e.tensor_copy(cur5[:, 16:17], par[:, bass.ds(i + PP["s5_d"][0], 1)]), "d")
                between()
                turns(2)
                turns(3)
                SGp.mark(e.tensor_copy(cur5[:, 18:19], cur5[:, 17:18]), "end")

            with e.Fori(0, DEPTH) as L:
                W.layer(L)
                lw = e.snap(L * N_LAYER + RAW + 2)
                e.wait_ge(lo_done, lw)
                W.settle()
                e.dma_start(par[:], params[L]).then_inc(par_in, 16)
                W.wait(LV, "prep_end")
                W.wait(LA, "prep_end")
                W.wait(LP, "k_rot")
                W.settle()
                LG.mark(e.memset(cz[:], 0.0), "cz0")
                W.wait(LG, "cz0")
                W.settle()
                LG.mark(e.memset(cur5[:], 0.0), "cur0")
                W.wait(LG, "cur0")
                W.settle()
                with e.Fori(0, 4) as I:
                    s5_tile(L, I, 0, lambda: None)
                with e.Fori(0, 4) as I:

                    def parameters(c):
                        W.tile(L, I, c)
                        i = I * 2 + c
                        W.wait(MV, "end", 2)
                        W.wait(MA, "end", 2)
                        W.wait(MG, "end", 1)
                        W.s5(L, I, 4)
                        W.wait(SGp, "end", 0 if c else 1)
                        cc = cur[:, c, :]
                        MG.mark(e.tensor_copy(cc[:, 16:24].rearrange("p (a b d) -> p a b d", a=2, b=2),
                                              dta[:, :, :, bass.ds(i * 2, 2)]), "cur1")
                        MG.mark(e.tensor_copy(cc[:, 24:26], par[:, bass.ds(i * 2 + PP["sinks"][0], 2)]), "cur2")
                        MG.mark(e.tensor_copy(cc[:, 27:28], par[:, bass.ds(i + PP["ssd_d"][0], 1)]), "cur4a")
                        MG.mark(e.tensor_copy(cc[:, 0:5], par[:, bass.ds(i * 5 + PP["conv"][0], 5)]), "cur5")
                        W.wait(MG, "cur4a")
                        W.settle()
                        MG.mark(e.tensor_scalar(cc[:, 27:28], cc[:, 27:28], 0.5, 0.0, ALU.mult, ALU.add), "cur4")

                    def values(c):
                        cc = cur[:, c, :]
                        W.tile(L, I, c)
                        if c == 0:
                            W.wait(MP, "A3_1", 1)
                            for r in range(2):
                                e.wait_ge(k_out, e.snap((L + 1) * 16))
                                W.settle()
                                e.dma_start(kcur[64 * r:64 * r + 64, :],
                                            kscr.rearrange("a (b p) t -> (a b) p t", b=2)[I]).then_inc(k_in, 16)
                            W.wait(SGp, "d")
                            MG.mark(e.tensor_copy(vcur[:], vt[:, :, bass.ds(I * 64, 64)]), "vcur")
                        else:
                            MG.mark(e.tensor_copy(cc[:, 28:29], cc[:, 24:25]), "vcur")
                        W.wait(MG, "vcur")
                        W.settle()
                        MG.mark(e.tensor_copy(cc[:, 29:30], cc[:, 27:28]), "end")

                    parameters(0)
                    W.wait(MG, "cur4")
                    s5_tile(L, I, 4, lambda: values(0))
                    parameters(1)
                    values(1)
                e.wait_ge(pair_done, e.snap(L * N_LAYER + N_BR + SPLIT))
                e.wait_ge(x_copied, 16)
                e.wait_ge(x_out, e.snap((L + 1) * 64))
                W.settle()
                e.dma_start(x_old[:], xs_out[L]).then_inc(x_back, 16)
                e.wait_ge(x_sum, e.snap(L * 17 + 18))
                W.wait(LP, "ss")
                W.settle()
                e.memset(ssum[:], 0.0).then_inc(x_sum, 1)
                with e.Fori(0, 4) as I:
                    for j in range(4):
                        e.wait_ge(x_sq, e.snap(L * 16 + I * 4 + (17 + j)))
                        e.wait_ge(x_sum, e.snap(L * 17 + I * 4 + (19 + j)))
                        W.settle()
                        e.tensor_tensor(ssum[:], ssum[:], proj[:, bass.ds(I * 4 + (16 + j), 1), :].rearrange("p a b -> p (a b)"),
                                        ALU.add).then_inc(x_sum, 1)

        @block.scalar
        def _(e):
            W = Where(e)
            for s in (LA, MA, SA):
                e.sem_inc(s.sem, 2 * s.n)
            e.sem_inc(merged_hi, 2)
            for s in spilled:
                e.sem_inc(s, 16)

            def hi(nb, j):
                if isinstance(nb, int):
                    e.wait_ge(landed[j % RAW], 16 * (j // RAW + 1))
                    e.wait_ge(pair_done, nb + (j + 1))
                else:
                    e.wait_ge(landed[j % RAW], nb[1] + 16 * (j // RAW))
                    e.wait_ge(pair_done, nb[0] + (j + 1))
                e.activation(w_hi[:, j % SPLIT, :], raw[:, j % RAW, :], ACT.Copy).then_inc(hi_done, 1)

            def start(L, off, I=None, g=0):
                if I is None:
                    return e.snap(L * N_LAYER + off), e.snap((L * (N_LAYER // RAW) + (off // RAW + 1)) * 16)
                return e.snap(L * N_LAYER + I * g + off), e.snap((L * (N_LAYER // RAW) + I * (g // RAW) + (off // RAW + 1)) * 16)

            def inv_sqrt(S_, name, out, logs, v, wait):
                wait()
                S_.mark(e.activation(logs, v, ACT.Ln), name + "_ln")
                W.wait(S_, name + "_ln")
                S_.mark(e.activation(out, logs, ACT.Exp, scale=-0.5), name + "_r")

            for m in range(KT):
                if m % 4 == 0:
                    e.wait_ge(x_in[m // 4], 16)
                e.activation(proj[:, 16 + m, :], proj[:, m, :], ACT.Square).then_inc(x_sq, 1)
            hi(0, 0)
            hi(0, 1)
            with e.Fori(0, DEPTH) as L:
                W.layer(L)
                e.wait_ge(pair_done, e.snap(L * N_LAYER + SPLIT))
                for q in range(4):
                    e.wait_ge(x_w, e.snap(L * 16 + (4 * q + 4)))
                    LA.mark(e.activation(h_hi[:, 4 * q:4 * q + 4, :], proj[:, 32 + 4 * q:36 + 4 * q, :], ACT.Copy), f"xhi{q}")
                inv_sqrt(LA, "rs", rstd[:], sv[:, 1, :], sv[:, 0, :], lambda: W.wait(LV, "rs_v"))
                nb = start(L, 0)
                for n in range(16):
                    hi(nb, n + 2)
                    if n == 0:
                        e.wait_ge(par_in, e.snap((L + 1) * 16))
                        LA.mark(e.activation(sp[:, 0, :], PR("log_dt", 0, ST), ACT.Exp), "s5_dt")
                        LA.mark(e.activation(sd[:, 6, 0:16], PR("a_log", 0, 16), ACT.Exp), "exp_a")
                        LA.mark(e.activation(wdt_hi[:], PR("w_dt", 0, KT * 16).rearrange("p (k c) -> p k c", k=KT), ACT.Copy), "wdt_hi")
                        LA.mark(e.activation(bgh[:], PR("b_glu", 0, BT), ACT.Copy, scale=0.5), "bgh")
                        W.wait(LV, "s5_ax")
                        LA.mark(e.activation(sp[:, 2, :], sp[:, 1, :], ACT.Tanh, scale=0.5), "s5_tanh")
                    if n == 1:
                        W.wait(LV, "turn_abs")
                        LA.mark(e.activation(sp[:, 5, :], sp[:, 3, :], ACT.Sin, scale=TWO_PI / 2), "s5_sin")
                        LA.mark(e.activation(sp[:, 6, :], sp[:, 4, :], ACT.Sin, scale=-TWO_PI / 2, bias=C("half_pi")), "s5_cos")
                    if n == 5:
                        W.wait(LV, "dt_abs")
                        LA.mark(e.activation(sd[:, 2, :], sd[:, 1, :], ACT.Exp, scale=-1.0), "dt_exp")
                    if n == 6:
                        W.wait(LV, "k_raw")
                        LA.mark(e.activation(kk[:, 0, :], kt[:].rearrange("p a b -> p (a b)"), ACT.Square), "k_sq")
                    if 4 <= n < 8:
                        t = n - 4
                        W.wait(LV, f"bc_conv{t}_3")
                        if t:
                            W.wait(LV, f"bc_silu{t - 1}")
                        LA.mark(e.activation(bt[:], kk[:, 2, 0:TOK] if t % 2 == 0 else kk[:, 2, TOK:], ACT.Tanh, scale=0.5), f"bc_tanh{t}")
                    if n == 8:
                        inv_sqrt(LA, "k", kk[:, 0, :], kk[:, 1, :], kk[:, 3, :], lambda: W.wait(LV, "k_v"))
                    if n == 13:
                        W.wait(LV, "k_fin")
                        e.dma_start(kscr.rearrange("a p t -> p a t"), kt[:]).then_inc(k_out, 16)
                        LA.mark(e.activation(small[:, 12:13], C("half_pi"), ACT.Copy), "prep_end")

                def sines(j):
                    W.wait(SGp, f"frac{j}")
                    W.wait(SV, f"q2_{j + 2}" if j < 2 else f"q2_{j - 2}", 1 if j < 2 else 0)
                    SA.mark(e.activation(tab[:, j % 2, 1, :], frac[:, j % 2, :], ACT.Sin, scale=TWO_PI), f"sin{j}")
                    W.wait(SA, f"cos{j - 1}" if j else "cos3", 0 if j else 1)
                    SA.mark(e.activation(zabs[:], frac[:, j % 2, :], ACT.Abs), f"abs{j}")
                    W.wait(SA, f"abs{j}")
                    SA.mark(e.activation(tab[:, j % 2, 0, :], zabs[:], ACT.Sin, scale=-TWO_PI, bias=C("half_pi")), f"cos{j}")

                def gelu_square():
                    W.wait(SV, "y5")
                    SA.mark(e.activation(t5[:], y5[:], ACT.Square), "y5sq")

                def gelu_tanh():
                    W.wait(SV, "g5b")
                    SA.mark(e.activation(t5[:], t5[:], ACT.Tanh, scale=GELU), "g5t")

                with e.Fori(0, 4) as I:
                    nb = start(L, N_IN, I, 8)
                    W.s5(L, I, 0)
                    for s in range(8):
                        hi(nb, s + 2)
                        if s == 0:
                            sines(0)
                            sines(1)
                        if s == 2:
                            sines(2)
                        if s == 4:
                            sines(3)
                        if s == 7:
                            gelu_square()
                            gelu_tanh()

                with e.Fori(0, 4) as I:
                    nb = start(L, N_GATE, I, 12)
                    W.s5(L, I, 4)
                    for c in range(2):
                        W.tile(L, I, c)
                        i = I * 2 + c
                        cc = cur[:, c, :]

                        def sum_decays(h):
                            W.wait(MG, "cur1")
                            W.wait(MP, "diff0" if h else "diff1", 0 if h else 1)
                            for q, (nm, b) in enumerate((("strict", 0), ("ones", 1), ("strict", 1))):
                                MA.mark(e.activation(m1[:, q, :], C(nm), ACT.Copy, scale=cc[:, 16 + 2 * b + h:17 + 2 * b + h]),
                                        f"m1_{h}{q}")

                        def head_exp(h):
                            W.wait(MP, f"diff{h}")
                            W.wait(MV, "ST1" if h == 0 else "ST0", 1 if h == 0 else 0)
                            MA.mark(e.activation(ex[:], b6[:, 0:384], ACT.Exp), f"ex{h}")

                        def att_exp(h):
                            W.wait(MV, f"nm{h}")
                            W.wait(MA, f"pn1{h ^ 1}", 0 if h else 1)
                            W.wait(MP, f"A2_{h ^ 1}", 0 if h else 1)
                            MA.mark(e.activation(pr[:, 0:128], sc[:, 0:128], ACT.Exp, bias=small[:, 2:3],
                                                 accum_out=small[:, 4:5]), f"pe0{h}")
                            MA.mark(e.activation(pr[:, 128:384], sc[:, 128:384], ACT.Exp, bias=small[:, 3:4],
                                                 accum_out=small[:, 5:6]), f"pe1{h}")
                            MA.mark(e.activation(small[:, 6:8], small[:, 2:4], ACT.Exp, bias=cc[:, 24 + h:25 + h]), f"pes{h}")

                        def att_norm(h):
                            W.wait(MV, f"rden{h}")
                            MA.mark(e.activation(pr[:, 0:128], pr[:, 0:128], ACT.Copy, scale=small[:, 10:11]), f"pn0{h}")
                            MA.mark(e.activation(pr[:, 128:384], pr[:, 128:384], ACT.Copy, scale=small[:, 11:12]), f"pn1{h}")

                        def pt_out(h):
                            W.wait(MP, f"A2_{h}")
                            W.wait(MP, f"A3_{h}", 1)
                            MA.mark(e.activation(pt[:, h], b5[:, 0:384], ACT.Copy), f"pt{h}")

                        for t in range(6):
                            s = 6 * c + t
                            if t == 4:
                                att_exp(1)
                            if t == 5:
                                pt_out(1)
                            hi(nb, s + 2)
                            if t == 0:
                                W.wait(MP, "q_ss", 1)
                                MA.mark(e.activation(tq[:], proj[:, bass.ds(i + Q, 1), :], ACT.Square), "q_sq")
                            if t == 4:
                                att_norm(1)
                            if t == 1:
                                inv_sqrt(MA, "q", qh[:], rq[:], rv[:], lambda: W.wait(MV, "q_v"))
                            W.wait(MV, f"gt{t}")
                            MA.mark(e.activation(gt[:, s % 4, :], gt[:, s % 4, :], ACT.Tanh, scale=0.5), f"gate{t}")
                            if t == 0:
                                W.wait(MV, "conv3")
                                MA.mark(e.activation(tt[:], xc[:], ACT.Tanh, scale=0.5), "xc_tanh")
                                sum_decays(0)
                            if s == 0:
                                sines(0)
                                sines(1)
                            if t == 2:
                                head_exp(0)
                                sum_decays(1)
                            if t == 3:
                                att_exp(0)
                                head_exp(1)
                                att_norm(0)
                            if t == 4:
                                pt_out(0)
                                MA.mark(e.activation(tz[:], proj[:, bass.ds(i + Z, 1), :], ACT.Tanh, scale=0.5), "tz")
                                MA.mark(e.activation(ta[:], proj[:, bass.ds(i + AG, 1), :], ACT.Tanh, scale=0.5), "ta")
                            if t == 5:
                                W.wait(MV, "yatt")
                                W.settle()
                                MA.mark(e.activation(ys[:, bass.ds(i + AG, 1), :], proj[:, bass.ds(i + Q, 1), :], ACT.Copy), "end")
                            if s == 5:
                                sines(2)
                            if s == 6:
                                sines(3)
                            if s == 11:
                                gelu_square()
                                gelu_tanh()

                W.last_tile(L)
                W.wait(SV, "s5g2")
                W.wait(MV, "end")
                W.wait(MP, "A3_1")
                W.wait(SGp, "end")
                for s in range(4):
                    e.wait_ge(spilled[s], e.snap((L * 12 + 13) * 16))
                nb = start(L, N_SG)

                def sg_tanh(j):
                    if j >= 2:
                        W.wait(LV, f"sg_b{j - 2}")
                    W.wait(LV, "sg_out")
                    LA.mark(e.activation(tsg[:, j % 2], proj[:, SG + 2 * j:SG + 2 * j + 2, :], ACT.Tanh, scale=0.5), f"sg_t{j}")

                def ssd_hi(q):
                    W.wait(LV, f"ssd_w{q}")
                    LA.mark(e.activation(ys[:, XS + 2 * q:XS + 2 * q + 2, :], proj[:, Z + 2 * q:Z + 2 * q + 2, :], ACT.Copy), f"ssd_hi{q}")

                def glu_hi(j):
                    W.wait(LV, f"glu_y{j}")
                    LA.mark(e.activation(ys[:, SG + 2 * j:SG + 2 * j + 2, :], proj[:, 2 * j:2 * j + 2, :], ACT.Copy), f"glu_hi{j}")

                for n in range(12):
                    hi(nb, n + 2)
                    if n == 1:
                        LA.mark(e.activation(g2_hi[:], proj[:, 0:BT, :], ACT.Copy), "g2_hi")
                    if 1 <= n < 5:
                        q = n - 1
                        if q >= 2:
                            W.wait(LP, f"ssd_ss{q - 2}")
                        LA.mark(e.activation(ssq[:, q % 2, :], proj[:, Z + 2 * q:Z + 2 * q + 2, :].rearrange("p a b -> p (a b)"),
                                             ACT.Square), f"ssd_sq{q}")
                    if n == 5:
                        inv_sqrt(LA, "ssd", acc[:, 0, :], nrm[:, 1, :], nrm[:, 0, :], lambda: W.wait(LV, "ssd_v"))
                    if n == 7:
                        sg_tanh(0)
                        ssd_hi(0)
                        ssd_hi(1)
                    if n >= 8:
                        j = n - 8
                        e.wait_ge(pair_done, nb[0] + (n + 3))
                        if j >= 2:
                            W.wait(LV, f"glu_y{j - 2}")
                        for a in range(2):
                            m = 2 * j + a
                            LA.mark(e.activation(tg[:, j % 2, a, :], mm[:, n % 2, a * 256:a * 256 + 256], ACT.Tanh, scale=0.25,
                                                 bias=bgh[:, m:m + 1]), f"glu_t{m}")
                        if j < 3:
                            sg_tanh(j + 1)
                        if j == 0:
                            ssd_hi(2)
                            ssd_hi(3)
                        else:
                            glu_hi(j - 1)
                glu_hi(3)
                W.wait(LV, "glu_lo3")
                with e.Fori(0, 2) as I:
                    nb = start(L, N_BR, I, 12)
                    for j in range(12):
                        hi(nb, j + 2)
                        for a in range(2):
                            u = 2 * j + a
                            if u % 3 == 2:
                                m = u // 3
                                e.wait_ge(merged, e.snap((L * 16 + I * 8 + (m + 1))))
                                W.settle()
                                e.activation(h_hi[:, bass.ds(I * 8 + m, 1), :], acc[:, m % 2, :], ACT.Copy).then_inc(merged_hi, 1)
                with e.Fori(0, 4) as I:
                    nb = start(L, N_OUT, I, 4)
                    for j in range(4):
                        hi(nb, j + 2)
                        e.wait_ge(x_new, e.snap(L * 16 + I * 4 + (j + 1)))
                        W.settle()
                        e.activation(proj[:, bass.ds(I * 4 + (16 + j), 1), :], proj[:, bass.ds(I * 4 + j, 1), :], ACT.Square).then_inc(x_sq, 1)
                    e.dma_start(xs_out[L + 1][:, bass.ds(I * 4, 4), :], proj[:, bass.ds(I * 4, 4), :]).then_inc(x_out, 16)

        @block.vector
        def _(e):
            W = Where(e)
            for s in (LV, MV, SV):
                e.sem_inc(s.sem, 2 * s.n)
            e.sem_inc(lo_done, RAW)
            e.sem_inc(summed, 5)

            def lo(nb, j):
                e.wait_ge(hi_done, nb + (j + 1))
                e.tensor_tensor(w_lo[:, j % SPLIT, :], raw[:, j % RAW, :], w_hi[:, j % SPLIT, :].bitcast(F32),
                                ALU.subtract).then_inc(lo_done, 1)

            def tt_(out, a, b, op):
                return e.tensor_tensor(out, a, b, op)

            def flat(a):
                return a.rearrange("p a b -> p (a b)")

            def newton(S, nm, y, t, v):
                W.wait(S_A[S], nm + "_r")
                S.mark(tt_(t, y, y, ALU.mult), nm + "_n1")
                W.wait(S, nm + "_n1")
                S.mark(tt_(t, t, v, ALU.mult), nm + "_n2")
                W.wait(S, nm + "_n2")
                S.mark(e.tensor_scalar(t, t, -0.5, 1.5, ALU.mult, ALU.add), nm + "_n3")
                W.wait(S, nm + "_n3")
                S.mark(tt_(y, y, t, ALU.mult), nm + "_n4")
                W.wait(S, nm + "_n4")

            S_A = {LV: LA, MV: MA}

            e.wait_ge(nw_in, 16)
            for m in range(KT):
                if m % 4 == 0:
                    e.wait_ge(x_in[m // 4], 16)
                e.tensor_scalar(proj[:, 32 + m, :], proj[:, m, :], nw[:, 0, m:m + 1], None, ALU.mult).then_inc(x_w, 1)
            lo(0, 0)
            lo(0, 1)
            with e.Fori(0, DEPTH) as L:
                W.layer(L)
                e.wait_ge(x_w, e.snap((L + 1) * 16))
                for q in range(4):
                    W.wait(LA, f"xhi{q}")
                    LV.mark(tt_(h_lo[:, 4 * q:4 * q + 4, :], proj[:, 32 + 4 * q:36 + 4 * q, :],
                                h_hi[:, 4 * q:4 * q + 4, :].bitcast(F32), ALU.subtract), f"xlo{q}")
                    if q == 0:
                        W.wait(LP, "ss")
                        LV.mark(e.tensor_scalar(sv[:, 0, :], b4[:, 0:TOK], 1.0 / D_MODEL, EPS, ALU.mult, ALU.add), "rs_v")
                newton(LV, "rs", rstd[:], sv[:, 1, :], sv[:, 0, :])

                count = [0]

                def chain(ins, name=None):
                    name = name or f"c{count[0]}"
                    count[0] += 1
                    LV.mark(ins, name)
                    W.wait(LV, name)

                def S(k):
                    return sp[:, k, :]
                a_re, a_im = PR("a_re", 0, ST), PR("a_im", 0, ST)

                def s5_angles():
                    e.wait_ge(par_in, e.snap((L + 1) * 16))
                    W.wait(LA, "s5_dt")
                    chain(tt_(S(1), a_re, S(0), ALU.mult), "s5_ax")
                    chain(tt_(S(3), a_im, S(0), ALU.mult))
                    chain(e.tensor_scalar(S(4), S(3), INV_2PI, ROUND, ALU.mult, ALU.add))
                    chain(e.tensor_scalar(S(4), S(4), ROUND, None, ALU.subtract))
                    for cpart in (C1, C2, C3):
                        chain(e.scalar_tensor_tensor(S(3), S(4), -cpart, S(3), ALU.mult, ALU.add))
                    chain(e.tensor_scalar(S(3), S(3), INV_2PI, 0.5, ALU.mult, ALU.min))
                    chain(e.tensor_scalar(S(3), S(3), -0.5, None, ALU.max))
                    chain(e.scalar_tensor_tensor(S(4), S(3), -1.0, S(3), ALU.mult, ALU.max), "turn_abs")
                    LV.mark(e.tensor_copy(s5p[:, 1, :], S(3)), "turns")
                    chain(e.tensor_copy(turn_hi[:], S(3)), "turn_hi")
                    LV.mark(e.tensor_copy(s5p[:, 2, :], turn_hi[:].bitcast(F32)), "turn_hi2")
                    LV.mark(tt_(s5p[:, 3, :], S(3), turn_hi[:].bitcast(F32), ALU.subtract), "turn_lo")

                def s5_gamma():
                    W.wait(LA, "s5_tanh")
                    chain(e.tensor_scalar(S(7), S(2), -1.0, 1.0, ALU.mult, ALU.add))
                    chain(e.reciprocal(S(8), S(7)))
                    chain(e.scalar_tensor_tensor(s5p[:, 0, :], S(2), 1.0, S(8), ALU.add, ALU.mult))
                    chain(e.scalar_tensor_tensor(S(9), S(2), 2.0, S(8), ALU.mult, ALU.mult))
                    W.wait(LA, "s5_cos")
                    chain(tt_(S(6), S(5), S(6), ALU.mult))
                    chain(tt_(S(5), S(5), S(5), ALU.mult))
                    chain(tt_(S(5), S(5), s5p[:, 0, :], ALU.mult))
                    chain(e.scalar_tensor_tensor(S(5), S(5), -2.0, S(9), ALU.mult, ALU.add))
                    chain(e.scalar_tensor_tensor(S(6), S(6), 2.0, s5p[:, 0, :], ALU.mult, ALU.mult))
                    chain(tt_(S(7), a_re, a_re, ALU.mult))
                    chain(tt_(S(8), a_im, a_im, ALU.mult))
                    chain(tt_(S(7), S(7), S(8), ALU.add))
                    chain(e.reciprocal(S(8), S(7)))
                    chain(tt_(S(9), S(5), a_re, ALU.mult))
                    chain(tt_(S(10), S(6), a_im, ALU.mult))
                    chain(tt_(S(9), S(9), S(10), ALU.add))
                    chain(tt_(S(9), S(9), S(8), ALU.mult))
                    chain(tt_(S(10), S(6), a_re, ALU.mult))
                    chain(tt_(S(11), S(5), a_im, ALU.mult))
                    chain(tt_(S(10), S(10), S(11), ALU.subtract))
                    chain(tt_(S(10), S(10), S(8), ALU.mult))

                c_re = PR("c_re", 0, ST * 16).rearrange("p (j h) -> p j h", h=16)
                c_im = PR("c_im", 0, ST * 16).rearrange("p (j h) -> p j h", h=16)
                g_re = S(9).unsqueeze(2).broadcast_to([P, ST, 16])
                g_im = S(10).unsqueeze(2).broadcast_to([P, ST, 16])
                ca = cw[:, 0, :].rearrange("p (j h) -> p j h", h=16)
                cb = cw[:, 1, :].rearrange("p (j h) -> p j h", h=16)

                def c_gamma(part):
                    if part == 0:
                        chain(tt_(ca, c_re, g_re, ALU.mult))
                        chain(tt_(cb, c_im, g_im, ALU.mult))
                        chain(tt_(ca, ca, cb, ALU.subtract))
                    else:
                        chain(tt_(cb, c_re, g_im, ALU.mult))
                        chain(tt_(c_re, c_im, g_re, ALU.mult))
                        chain(e.scalar_tensor_tensor(c_im, cb, -1.0, c_re, ALU.mult, ALU.subtract))
                        chain(e.tensor_copy(c_re, ca))

                def D(k):
                    return sd[:, k, :]

                def dt_softplus():
                    W.wait(LA, "dt_exp")
                    chain(e.tensor_scalar(D(3), D(2), 2.0, None, ALU.add))
                    chain(e.reciprocal(D(4), D(3)))
                    chain(tt_(D(3), D(2), D(4), ALU.mult))
                    chain(tt_(D(4), D(3), D(3), ALU.mult))
                    chain(e.tensor_scalar(D(5), D(4), 1.0 / 17, None, ALU.mult))
                    for k in (15, 13, 11, 9, 7, 5, 3):
                        chain(e.scalar_tensor_tensor(D(5), D(5), 1.0 / k, D(4), ALU.add, ALU.mult))
                    chain(e.scalar_tensor_tensor(D(5), D(5), 1.0, D(3), ALU.add, ALU.mult))
                    chain(e.tensor_scalar(D(1), D(0), 0.0, None, ALU.max))
                    chain(e.scalar_tensor_tensor(D(7), D(5), 2.0, D(1), ALU.mult, ALU.add))
                    chain(e.tensor_scalar(flat(dta[:, 1]), D(7), 0.5, None, ALU.mult))
                    chain(e.scalar_tensor_tensor(dta[:, 0], D(7).rearrange("p (a b) -> p a b", a=2), -1.0,
                                                 sd[:, 6, 0:16].unsqueeze(1).broadcast_to([P, 2, 16]), ALU.mult, ALU.mult))

                def conv(dst, src, wcol, S_, nm):
                    S_.mark(e.tensor_scalar(dst, src, wcol(3), wcol(4), ALU.mult, ALU.add), nm + "0")
                    for sft in range(1, 4):
                        W.wait(S_, nm + f"{sft - 1}")
                        S_.mark(e.scalar_tensor_tensor(dst[:, sft:TOK], src[:, 0:TOK - sft], wcol(3 - sft), dst[:, sft:TOK],
                                                       ALU.mult, ALU.add), nm + f"{sft}")

                def bc_dst(t):
                    return kk[:, 2, 0:TOK] if t % 2 == 0 else kk[:, 2, TOK:]

                ktf = flat(kt[:])

                def twice(a):
                    return a.unsqueeze(1).broadcast_to([P, 2, TOK])

                def two(a):
                    return a.rearrange("p (a b) -> p a b", a=2)

                nb = e.snap(L * N_LAYER)
                for n in range(16):
                    if n == 8:
                        e.wait_ge(x_out, e.snap((L + 1) * 64))
                        W.settle()
                    e.wait_ge(pair_done, nb + (n + 3))
                    bank = mm[:, n % 2, 0:256]
                    if n < 4:
                        LV.mark(tt_(proj[:, BC + n, :], bank, rstd[:], ALU.mult), f"in{n}")
                    elif n < 6:
                        LV.mark(tt_(kt[:, n - 4, :], bank, rstd[:], ALU.mult), "k_raw" if n == 5 else "in4")
                    elif n < 8:
                        for t in range(2):
                            ins = e.tensor_scalar(vt[:, t, (n - 6) * 128:(n - 5) * 128], mm[:, n % 2, t * 128:t * 128 + 128],
                                                  rtok[:, t:t + 1], None, ALU.mult)
                        LV.mark(ins, f"in{n}")
                    else:
                        LV.mark(tt_(proj[:, U + n - 8, :], bank, rstd[:], ALU.mult), f"in{n}")
                    if n == 4:
                        W.wait(LP, "dt_t")
                        LV.mark(tt_(sv[0:16, 0, :], b6[0:16, 0:256], rstd[0:16, :], ALU.mult), "dt_s")
                    lo(nb, n + 2)
                    if n == 0:
                        s5_angles()
                    if n == 1:
                        W.wait(LP, "rtok")
                        chain(e.tensor_copy(rtok[:], b5[:, 0:2]), "rtok")
                        W.wait(LA, "wdt_hi")
                        LV.mark(tt_(wdt_lo[:], PR("w_dt", 0, KT * 16).rearrange("p (k c) -> p k c", k=KT), wdt_hi[:].bitcast(F32),
                                    ALU.subtract), "wdt_lo")
                    if n == 2:
                        s5_gamma()
                    if n in (3, 4):
                        c_gamma(n - 3)
                    if n == 5:
                        W.wait(LP, "dt")
                        for t in range(2):
                            LV.mark(tt_(sd[:, 0, t * 16:t * 16 + 16], b6[:, 256 + t * 16:272 + t * 16], PR("dt_bias", 0, 16), ALU.add),
                                    f"dt_x{t}")
                        W.wait(LV, "dt_x1")
                        chain(e.scalar_tensor_tensor(D(1), D(0), -1.0, D(0), ALU.mult, ALU.max), "dt_abs")
                    if 5 <= n < 9:
                        t = n - 5
                        W.wait(LA, f"bc_tanh{t}")
                        LV.mark(e.scalar_tensor_tensor(proj[:, BC + t, :], bt[:], 1.0, bc_dst(t), ALU.add, ALU.mult), f"bc_silu{t}")
                    if 4 <= n < 8:
                        t = n - 4
                        W.wait(LV, f"in{t}")
                        conv(bc_dst(t), proj[:, BC + t, :], lambda k, t=t: PR("conv", (8 + t) * 5 + k), LV, f"bc_conv{t}_")
                    if n == 6:
                        dt_softplus()
                    if n == 8:
                        W.wait(LP, "k_ss")
                        LV.mark(e.tensor_scalar(kk[:, 3, :], b7[:], 1.0 / HD, EPS, ALU.mult, ALU.add), "k_v")
                    if n == 9:
                        newton(LV, "k", kk[:, 0, :], kk[:, 1, :], kk[:, 3, :])
                        chain(e.scalar_tensor_tensor(kk[:, 1, :], ktf, PR("k_norm"), kk[:, 0, :], ALU.mult, ALU.mult), "kn")
                    if n == 10:
                        for g in range(2):
                            W.wait(LP, f"G{g}")
                            b = (b4, b5)[g]
                            tri = C("tri", P)
                            LV.mark(e.scalar_tensor_tensor(gm[:, g, 0:128], b[:, 0:128], 0.25, tri, ALU.mult, ALU.mult), f"gm{g}0")
                            LV.mark(e.tensor_scalar(gm[:, g, 128:256], b[:, 128:256], 0.25, None, ALU.mult), f"gm{g}1")
                            LV.mark(e.scalar_tensor_tensor(gm[:, g, 256:384], b[:, 256:384], 0.25, tri, ALU.mult, ALU.mult), f"gm{g}2")
                    if n == 12:
                        LV.mark(tt_(two(kk[:, 0, :]), two(kk[:, 1, :]), twice(C("cos")), ALU.mult), "k_c")
                        W.wait(LP, "k_rot")
                        chain(tt_(two(kk[:, 3, :]), two(b6[:]), twice(C("sin")), ALU.mult))
                        chain(tt_(ktf, kk[:, 0, :], kk[:, 3, :], ALU.add), "k_fin")
                        chain(e.tensor_scalar(small[:, 9:10], C("half_pi"), 0.0, None, ALU.mult), "prep_end")
                W.wait(LV, "in15")
                W.settle()

                def s5_halves(I, more):
                    bu = b4[:].rearrange("p (a b) -> p a b", a=2)
                    p2 = prod2[:]

                    def back(j):
                        p1 = prod[:, j % 2]
                        W.wait(SP, f"bu{j}")
                        W.wait(SA, f"cos{j}")
                        W.wait(SP, f"C{j - 2}" if j >= 2 else f"C{j + 2}", 0 if j >= 2 else 1)
                        SV.mark(tt_(p1, bu, tab[:, j % 2, 0, :].unsqueeze(1).broadcast_to([P, 2, TOK]), ALU.mult), f"p1_{j}")
                        W.wait(SV, f"sim{j - 1}" if j else "sim3", 0 if j else 1)
                        SV.mark(tt_(p2, bu, tab[:, j % 2, 1, :].unsqueeze(1).broadcast_to([P, 2, TOK]), ALU.mult), f"p2_{j}")

                    def inputs(j):
                        p1 = prod[:, j % 2]
                        W.wait(SV, f"p2_{j}")
                        SV.mark(tt_(p1[:, 0, :], p1[:, 0, :], p2[:, 1, :], ALU.add), f"vre{j}")
                        SV.mark(tt_(p1[:, 1, :], p1[:, 1, :], p2[:, 0, :], ALU.subtract), f"vim{j}")

                    def scan(j):
                        p1 = prod[:, j % 2]
                        if j == 0:
                            W.wait(SGp, "d")
                        dec = cur5[:, 12 + j:13 + j].broadcast_to([P, TOK])
                        W.wait(SV, f"vre{j}")
                        SV.mark(e.tensor_tensor_scan(wst[:, 0, :], dec, p1[:, 0, :], 0.0, ALU.mult, ALU.add), f"wre{j}")
                        W.wait(SV, f"vim{j}")
                        SV.mark(e.tensor_tensor_scan(wst[:, 1, :], dec, p1[:, 1, :], 0.0, ALU.mult, ALU.add), f"wim{j}")

                    def forth(j):
                        W.wait(SV, f"wim{j}")
                        SV.mark(tt_(prod[:, j % 2], wst[:], tab[:, j % 2, 0, :].unsqueeze(1).broadcast_to([P, 2, TOK]), ALU.mult), f"q1_{j}")
                        SV.mark(tt_(p2, wst[:], tab[:, j % 2, 1, :].unsqueeze(1).broadcast_to([P, 2, TOK]), ALU.mult), f"q2_{j}")

                    def states(j):
                        p1 = prod[:, j % 2]
                        W.wait(SV, f"q2_{j}")
                        SV.mark(tt_(p1[:, 0, :], p1[:, 0, :], p2[:, 1, :], ALU.subtract), f"sre{j}")
                        SV.mark(tt_(p1[:, 1, :], p1[:, 1, :], p2[:, 0, :], ALU.add), f"sim{j}")

                    u = flat(proj[:, bass.ds(I + (U + more), 1), :])

                    def out():
                        W.wait(SP, "C3")
                        SV.mark(e.scalar_tensor_tensor(y5[:], u, cur5[:, 16:17], ps_s5, ALU.mult, ALU.add), "y5")

                    def gelu_inner():
                        W.wait(SA, "y5sq")
                        SV.mark(e.tensor_scalar(t5[:], t5[:], 0.044715, 1.0, ALU.mult, ALU.add), "g5a")
                        W.wait(SV, "g5a")
                        SV.mark(tt_(t5[:], t5[:], y5[:], ALU.mult), "g5b")

                    def gelu():
                        W.wait(SA, "g5t")
                        SV.mark(e.scalar_tensor_tensor(u, t5[:], 1.0, y5[:], ALU.add, ALU.mult), "s5g2")

                    return back, inputs, scan, forth, states, out, gelu_inner, gelu

                with e.Fori(0, 4) as I:
                    nb = e.snap(L * N_LAYER + N_IN + I * 8)
                    W.s5(L, I, 0)
                    back, inputs, scan, forth, states, out, gelu_inner, gelu = s5_halves(I, 0)
                    for s in range(8):
                        e.wait_ge(pair_done, nb + (s + 3))
                        tt_(flat(proj[:, bass.ds(I * 8 + (16 + s), 1), :]), mm[:, s % 2, 0:256], rstd[:], ALU.mult)
                        if s == 1:
                            scan(0)
                        if s == 2:
                            back(1)
                        if s == 3:
                            forth(1)
                        if s == 4:
                            inputs(2)
                            scan(2)
                        if s == 5:
                            back(3)
                        if s == 6:
                            forth(3)
                        if s == 7:
                            out()
                        lo(nb, s + 2)
                        if s == 0:
                            back(0)
                            inputs(0)
                        if s == 1:
                            forth(0)
                            states(0)
                        if s == 2:
                            inputs(1)
                            scan(1)
                        if s == 3:
                            states(1)
                            back(2)
                        if s == 4:
                            forth(2)
                            states(2)
                        if s == 5:
                            inputs(3)
                            scan(3)
                        if s == 6:
                            states(3)
                        if s == 7:
                            gelu_inner()
                            gelu()

                e.wait_ge(lo_done, e.snap(L * N_LAYER + N_GATE + 2 + RAW))
                W.settle()
                with e.Fori(0, 4) as I:
                    nb = e.snap(L * N_LAYER + N_GATE + I * 12)
                    sb0 = e.snap((L * 12 + I * 3 + 1) * 16)
                    W.s5(L, I, 4)
                    back, inputs, scan, forth, states, out, gelu_inner, gelu = s5_halves(I, 4)
                    for c in range(2):
                        W.tile(L, I, c)
                        i = I * 2 + c
                        cc = cur[:, c, :]

                        def slot(k):
                            return flat(proj[:, bass.ds(i + k, 1), :])

                        def st_make(h):
                            W.wait(MA, f"ex{h}")
                            W.wait(MP, "ys0" if h else "ys1", 0 if h else 1)
                            MV.mark(tt_(stt_[:], ex[:], flat(gm[:, bass.ds(I // 2, 1), :]), ALU.mult), f"ST{h}")

                        def att_scores(h):
                            W.wait(MP, f"A1_{h}")
                            W.wait(MA, "pes0" if h else "pes1", 0 if h else 1)
                            MV.mark(e.scalar_tensor_tensor(sc[:], b7[:, 0:384], HD ** -0.5, C("amask"), ALU.mult, ALU.add), f"sc{h}")
                            W.wait(MV, f"sc{h}")
                            W.wait(MV, f"den{h ^ 1}", 0 if h else 1)
                            MV.mark(e.tensor_reduce(small[:, 0:1], sc[:, 0:128], AX.X, ALU.max), f"mx0{h}")
                            MV.mark(e.tensor_reduce(small[:, 1:2], sc[:, 128:384], AX.X, ALU.max), f"mx1{h}")
                            W.wait(MV, f"mx1{h}")
                            MV.mark(e.tensor_scalar(small[:, 2:4], small[:, 0:2], cc[:, 24 + h:25 + h], -1.0, ALU.max, ALU.mult), f"nm{h}")

                        def att_sum(h):
                            W.wait(MA, f"pes{h}")
                            MV.mark(tt_(small[:, 6:8], small[:, 6:8], small[:, 4:6], ALU.add), f"den{h}")
                            W.wait(MV, f"den{h}")
                            W.wait(MA, "pn10" if h else "pn11", 0 if h else 1)
                            MV.mark(e.reciprocal(small[:, 10:12], small[:, 6:8]), f"rden{h}")

                        for t in range(6):
                            s = 6 * c + t
                            e.wait_ge(pair_done, nb + (s + 3))
                            e.wait_ge(spilled[s % 4], sb0 + 16 * (s // 4))
                            MV.mark(tt_(gt[:, s % 4, :], mm[:, s % 2, 0:256], rstd[:], ALU.mult), f"gt{t}")
                            if t == 0:
                                W.wait(MG, "cur5")
                                W.wait(MP, "xT", 1)
                                conv(xc[:], slot(XS), lambda k: cc[:, k:1 + k], MV, "conv")
                            if t == 1:
                                W.wait(MP, "q_ss")
                                MV.mark(e.tensor_scalar(rv[:], b7[:, 0:256], 1.0 / HD, EPS, ALU.mult, ALU.add), "q_v")
                                W.wait(MP, "xT")
                                W.wait(MP, "ys1", 1)
                                W.wait(MG, "cur1")
                                MV.mark(tt_(xdt[:], b6[:, 0:256].rearrange("p (a h d) -> p a h d", a=2, h=2),
                                            cc[:, 20:24].rearrange("p (a h) -> p a h", a=2).unsqueeze(3).broadcast_to([P, 2, 2, 64]),
                                            ALU.mult), "xdt")
                            if t == 3:
                                att_scores(0)
                            if s == 4:
                                states(0)
                            if s == 10:
                                inputs(3)
                            if t == 4:
                                att_sum(1)
                            if s == 10:
                                scan(3)
                            if t == 5:
                                W.wait(MA, "tz")
                                MV.mark(e.scalar_tensor_tensor(tz[:], tz[:], 1.0, slot(Z), ALU.add, ALU.mult), "zb")
                                W.wait(MA, "ta")
                                MV.mark(e.scalar_tensor_tensor(ta[:], ta[:], 1.0, slot(AG), ALU.add, ALU.mult), "ab")
                                W.wait(MP, "A3_1")
                                W.wait(MV, "ab")
                                MV.mark(e.scalar_tensor_tensor(slot(Q), ps_att, 0.5, ta[:], ALU.mult, ALU.mult), "yatt")
                            if s == 11:
                                out()
                            lo(nb, s + 2)
                            if t == 0:
                                W.wait(MA, "xc_tanh")
                                MV.mark(e.scalar_tensor_tensor(xc[:], tt[:], 1.0, xc[:], ALU.add, ALU.mult), "xc")
                            if t == 2:
                                W.wait(MV, "qn")
                                MV.mark(tt_(qh[:], qn[:], C("cos"), ALU.mult), "q_c")
                                st_make(0)
                                W.wait(MP, "q_rot")
                                MV.mark(tt_(rq[:], b7[:, 256:512], C("sin"), ALU.mult), "q_s")
                                W.wait(MV, "q_s")
                                MV.mark(tt_(qh[:], qh[:], rq[:], ALU.add), "qh")
                            if t == 3:
                                att_sum(0)
                                st_make(1)
                                att_scores(1)
                            if t == 4:
                                W.wait(MP, "ys1")
                                W.wait(MG, "cur4")
                                MV.mark(e.scalar_tensor_tensor(xc[:], xc[:], cc[:, 27:28], ps_ssd, ALU.mult, ALU.add), "yv")
                            if t == 5:
                                MV.mark(e.scalar_tensor_tensor(slot(Z), xc[:], 0.5, tz[:], ALU.mult, ALU.mult), "yz")
                                W.wait(MA, "end")
                                MV.mark(tt_(flat(ys[:, bass.ds(i + Q, 1), :]), slot(Q),
                                            flat(ys[:, bass.ds(i + AG, 1), :]).bitcast(F32), ALU.subtract), "end")
                            if s == 1:
                                back(0)
                            if s == 2:
                                inputs(0)
                                scan(0)
                            if s == 3:
                                forth(0)
                            if s == 4:
                                back(1)
                                inputs(1)
                            if s == 5:
                                scan(1)
                                forth(1)
                            if s == 6:
                                states(1)
                                back(2)
                            if s == 7:
                                inputs(2)
                            if s == 8:
                                scan(2)
                                forth(2)
                                states(2)
                            if s == 9:
                                back(3)
                            if s == 10:
                                forth(3)
                                states(3)
                            if t == 1:
                                newton(MV, "q", qh[:], rq[:], rv[:])
                                W.wait(MP, "q_rot", 1)
                                MV.mark(e.scalar_tensor_tensor(qn[:], slot(Q), PR("q_norm"), qh[:], ALU.mult, ALU.mult), "qn")
                            if s == 11:
                                gelu_inner()
                                gelu()

                W.last_tile(L)
                W.wait(MP, "A3_1")
                W.wait(SGp, "end")
                W.wait(MG, "end")
                nb = e.snap(L * N_LAYER + N_SG)

                def ssd_lo(q):
                    W.wait(LA, f"ssd_hi{q}")
                    LV.mark(tt_(ys[:, Z + 2 * q:Z + 2 * q + 2, :], proj[:, Z + 2 * q:Z + 2 * q + 2, :],
                                ys[:, XS + 2 * q:XS + 2 * q + 2, :].bitcast(F32), ALU.subtract), f"ssd_lo{q}")

                def glu_lo(j):
                    W.wait(LA, f"glu_hi{j}")
                    LV.mark(tt_(ys[:, 2 * j:2 * j + 2, :], proj[:, 2 * j:2 * j + 2, :],
                                ys[:, SG + 2 * j:SG + 2 * j + 2, :].bitcast(F32), ALU.subtract), f"glu_lo{j}")

                for n in range(12):
                    if n < 8:
                        e.wait_ge(pair_done, nb + (n + 3))
                        LV.mark(tt_(proj[:, SG + n, :], mm[:, n % 2, 0:256], rstd[:], ALU.mult), "sg_out" if n == 7 else f"sg{n}")
                    else:
                        if n == 9:
                            ssd_lo(2)
                            ssd_lo(3)
                        j = n - 8
                        pairs = slice(SG + 2 * j, SG + 2 * j + 2)
                        W.wait(LA, f"sg_t{j}")
                        LV.mark(e.scalar_tensor_tensor(proj[:, pairs, :], tsg[:, j % 2], 1.0, proj[:, pairs, :], ALU.add, ALU.mult), f"sg_b{j}")
                        W.wait(LA, f"glu_t{2 * j + 1}")
                    lo(nb, n + 2)
                    if n == 2:
                        W.wait(LA, "g2_hi")
                        LV.mark(tt_(g2_lo[:], proj[:, 0:BT, :], g2_hi[:].bitcast(F32), ALU.subtract), "g2_lo")
                    if n == 5:
                        for s in range(4):
                            e.wait_ge(spilled[s], e.snap((L * 12 + 13) * 16))
                            W.settle()
                        W.wait(LP, "ssd_ss3")
                        LV.mark(e.tensor_scalar(nrm[:, 0, :], b4[:, 0:256], 1.0 / BW, EPS, ALU.mult, ALU.add), "ssd_v")
                    if n == 6:
                        newton(LV, "ssd", acc[:, 0, :], nrm[:, 1, :], nrm[:, 0, :])
                    if n in (6, 7):
                        for m in range(4 * n - 24, 4 * n - 20):
                            LV.mark(e.scalar_tensor_tensor(proj[:, Z + m, :], proj[:, Z + m, :], PR("ssd_norm", m), acc[:, 0, :],
                                                           ALU.mult, ALU.mult), f"ssd_w{m // 2}" if m % 2 else f"ssd_w_{m}")
                    if n == 8:
                        ssd_lo(0)
                        ssd_lo(1)
                    if n >= 8:
                        LV.mark(e.scalar_tensor_tensor(tg[:, j % 2], tg[:, j % 2], 1.0, proj[:, 2 * j:2 * j + 2, :], ALU.add, ALU.mult), f"glu_a{j}")
                        W.wait(LV, f"glu_a{j}")
                        W.wait(LV, f"sg_b{j}")
                        LV.mark(e.scalar_tensor_tensor(proj[:, 2 * j:2 * j + 2, :], tg[:, j % 2], 0.125, proj[:, pairs, :],
                                                       ALU.mult, ALU.mult), f"glu_y{j}")
                        if j:
                            glu_lo(j - 1)
                glu_lo(3)

                W.settle()
                with e.Fori(0, 2) as I:
                    nb = e.snap(L * N_LAYER + N_BR + I * 12)
                    mb = e.snap(L * 16 + I * 8)
                    gb = e.snap((L * 12 + I * 6 + 1) * 16)
                    sb_ = e.snap(L * 80 + I * 40)
                    for j in range(12):
                        e.wait_ge(pair_done, nb + (j + 3))
                        e.wait_ge(gate_in[j % 2], gb + 16 * (j // 2))
                        for a in range(2):
                            u = 2 * j + a
                            m, b = u // 3, u % 3
                            k = 5 * m
                            dst = acc[:, m % 2, :] if b == 0 else tmp[:]
                            if b == 0:
                                e.wait_ge(merged_hi, mb + (m + 1))
                            else:
                                e.wait_ge(summed, sb_ + (k + (5, 8)[b - 1]))
                            ins = e.scalar_tensor_tensor(dst, gin[:, j % 2, a, :], 1.0, mm[:, j % 2, a * 256:a * 256 + 256], ALU.add, ALU.mult)
                            ins.then_inc(summed, 1)
                            if b:
                                e.wait_ge(summed, sb_ + (k + 2 * b + 5))
                                ins = tt_(acc[:, m % 2, :], acc[:, m % 2, :], tmp[:], ALU.add)
                                ins.then_inc(summed, 1)
                            if b == 2:
                                e.wait_ge(summed, sb_ + (k + 5 + 5))
                                e.tensor_scalar(acc[:, m % 2, :], acc[:, m % 2, :], 0.5, None, ALU.mult).then_inc(merged, 1)
                        lo(nb, j + 2)
                        for a in range(2):
                            u = 2 * j + a
                            m, b = u // 3, u % 3
                            if b == 2:
                                e.wait_ge(merged_hi, mb + (m + 3))
                                tt_(flat(h_lo[:, bass.ds(I * 8 + m, 1), :]), acc[:, m % 2, :],
                                    flat(h_hi[:, bass.ds(I * 8 + m, 1), :]).bitcast(F32), ALU.subtract).then_inc(merged_lo, 1)

                W.settle()
                e.wait_ge(nw_pad, 1)
                with e.Fori(0, 4) as I:
                    nb = e.snap(L * N_LAYER + N_OUT + I * 4)
                    e.wait_ge(x_back, e.snap((L + 1) * 16))
                    for j in range(4):
                        e.wait_ge(pair_done, nb + (j + 3))
                        x_tile = flat(proj[:, bass.ds(I * 4 + j, 1), :])
                        tt_(x_tile, mm[:, j % 2, 0:256], flat(x_old[:, bass.ds(I * 4 + j, 1), :]), ALU.add).then_inc(x_new, 1)
                        e.wait_ge(x_new, e.snap(L * 16 + I * 4 + (j + 1)))
                        W.settle()
                        e.tensor_scalar(flat(proj[:, bass.ds(I * 4 + j + 32, 1), :]), x_tile,
                                        flat(nw[:, bass.ds(L + 1, 1), bass.ds(I * 4 + j, 1)]), None, ALU.mult).then_inc(x_w, 1)
                        lo(nb, j + 2)

        @block.tensor
        def _(e):
            W = Where(e)
            for s in (LP, MP, SP):
                e.sem_inc(s.sem, 2 * s.n)
            e.sem_inc(pair_done, SPLIT)

            def prod3(out, whi, wlo, xhi, xlo, start, stop):
                e.matmul(out, whi, xlo, start=start, stop=False)
                e.matmul(out, wlo, xhi, start=False, stop=False)
                return e.matmul(out, whi, xhi, start=False, stop=stop)

            def pair(nb, j, before=None):
                e.wait_ge(lo_done, nb + (j + 1 + RAW))
                for k in range(KT):
                    if before and k % 4 == 0:
                        before(k // 4)
                    w = slice(k * P, k * P + P)
                    ins = prod3(mm[:, j % 2, 0:256], w_hi[:, j % 2, w], w_lo[:, j % 2, w], h_hi[:, k, :], h_lo[:, k, :],
                                k == 0, k == KT - 1)
                ins.then_inc(pair_done, 1)

            def units(nb, j, sides, before=None):
                e.wait_ge(lo_done, nb + (j + 1 + RAW))
                for a in (1, 0) if before else (0, 1):
                    if before and a == 0:
                        before()
                    xhi, xlo = sides[a]
                    for k in range(BT):
                        w = slice((a * BT + k) * P, (a * BT + k + 1) * P)
                        ins = prod3(mm[:, j % 2, a * 256:a * 256 + 256], w_hi[:, j % 2, w], w_lo[:, j % 2, w],
                                    xhi[:, k, :], xlo[:, k, :], k == 0, k == BT - 1)
                ins.then_inc(pair_done, 1)

            e.wait_ge(const_in, 16)
            with e.Fori(0, DEPTH) as L:
                W.layer(L)
                xs = e.snap(L * 17 + 18)

                def first(q):
                    if q == 0:
                        e.wait_ge(x_sum, xs)
                        LP.mark(e.matmul(b4[:, 0:TOK], C("ones"), ssum[:], start=True, stop=True), "ss")
                    W.wait(LV, f"xlo{q}")

                nb = e.snap(L * N_LAYER)
                for n in range(16):
                    if n in (6, 7):
                        e.wait_ge(lo_done, nb + (n + 1 + RAW))
                        for t in range(2):
                            for k in range(KT):
                                w, tok = slice(k * P, k * P + P), slice(t * P, t * P + P)
                                ins = prod3(mm[:, n % 2, tok], h_hi[:, k, tok], h_lo[:, k, tok], w_hi[:, n % 2, w], w_lo[:, n % 2, w],
                                            k == 0, k == KT - 1)
                        ins.then_inc(pair_done, 1)
                    else:
                        pair(nb, n, first if n == 0 else None)
                    if n == 0:
                        W.wait(LV, "rs_n4")
                        for t in range(2):
                            ins = e.matmul(b5[:, t:t + 1], rstd[:, t * P:t * P + P], C("ident", 1), start=True, stop=True)
                        LP.mark(ins, "rtok")
                    if n == 3:
                        W.wait(LV, "wdt_lo")
                        for k in range(KT):
                            ins = prod3(b6[0:16, 0:256], wdt_hi[:, k, :], wdt_lo[:, k, :], h_hi[:, k, :], h_lo[:, k, :],
                                        k == 0, k == KT - 1)
                        LP.mark(ins, "dt_t")
                    if n == 5:
                        W.wait(LV, "dt_s")
                        W.settle()
                        for t in range(2):
                            ins = e.matmul(b6[:, 256 + t * 16:272 + t * 16], sv[0:16, 0, t * P:t * P + P], C("ident")[0:16, 0:16],
                                           start=True, stop=True)
                        LP.mark(ins, "dt")
                    if n == 7:
                        W.wait(LA, "k_sq")
                        LP.mark(e.matmul(b7[:], C("blk"), kk[:, 0, :], start=True, stop=True), "k_ss")
                    if n == 9:
                        W.wait(LV, "bc_silu3")
                        for g in range(2):
                            b = (b4, b5)[g]
                            e.matmul(b[:, 0:256], proj[:, BC + g, 0:P], proj[:, BC + 2 + g, :], start=True, stop=True)
                            LP.mark(e.matmul(b[:, 256:384], proj[:, BC + g, P:TOK], proj[:, BC + 2 + g, P:TOK], start=True, stop=True), f"G{g}")
                    if n == 11:
                        W.wait(LV, "kn")
                        LP.mark(e.matmul(b6[:], C("rot"), kk[:, 1, :], start=True, stop=True), "k_rot")

                def s5_products(I, more):
                    def bu(j):
                        W.wait(SGp, "bz1")
                        W.wait(SV, f"p2_{j - 1}" if j else "p2_3", 0 if j else 1)
                        for r in range(2):
                            ins = e.matmul(b4[:, r * 256:r * 256 + 256],
                                           bz[:, r, 2 * j:2 * j + 2, :].rearrange("p a b -> p (a b)"),
                                           proj[:, bass.ds(I + (U + more), 1), :].rearrange("p a b -> p (a b)"), start=True, stop=True)
                        SP.mark(ins, f"bu{j}")

                    def cs(j):
                        if j == 0:
                            W.wait(SGp, "cz11")
                            W.wait(SV, "y5", 1)
                        W.wait(SV, f"sim{j}")
                        for r in range(2):
                            ins = e.matmul(ps_s5[32 * j:32 * j + 32, :], cz[:, j, r, :], prod[:, j % 2, r, :],
                                           start=r == 0, stop=r == 1)
                        SP.mark(ins, f"C{j}")

                    return bu, cs

                W.settle()
                with e.Fori(0, 4) as I:
                    nb = e.snap(L * N_LAYER + N_IN + I * 8)
                    W.s5(L, I, 0)
                    bu, cs = s5_products(I, 0)
                    for s in range(8):
                        pair(nb, s)
                        if s == 0:
                            bu(0)
                        if s == 1:
                            bu(1)
                        if s == 2:
                            cs(0)
                        if s == 3:
                            bu(2)
                        if s == 4:
                            cs(1)
                            bu(3)
                        if s == 5:
                            cs(2)
                        if s == 7:
                            cs(3)

                W.settle()
                with e.Fori(0, 4) as I:
                    nb = e.snap(L * N_LAYER + N_GATE + I * 12)
                    W.s5(L, I, 4)
                    keys = e.snap((L * 4 + I + 1) * 32)
                    bu, cs = s5_products(I, 4)
                    for c in range(2):
                        W.tile(L, I, c)
                        i = I * 2 + c

                        def diff(h):
                            W.wait(MA, f"m1_{h}2")
                            W.wait(MA, f"ex{h ^ 1}", 0 if h else 1)
                            if not h:
                                W.wait(MV, "xdt")
                            e.matmul(b6[:, 0:256], m1[:, 0, :], C("tri"), start=True, stop=False)
                            e.matmul(b6[:, 128:256], m1[:, 1, :], C("tri", P), start=False, stop=True)
                            MP.mark(e.matmul(b6[:, 256:384], m1[:, 2, :], C("tri", P), start=True, stop=True), f"diff{h}")

                        def ssd_y(h):
                            W.wait(MV, f"ST{h}")
                            if not h:
                                W.wait(MV, "yatt", 1)
                            rows = slice(64 * h, 64 * h + 64)
                            e.matmul(ps_ssd[rows, :], xdt[:, 0, h, :], stt_[:, 0:256], start=True, stop=False)
                            MP.mark(e.matmul(ps_ssd[rows, 128:256], xdt[:, 1, h, :], stt_[:, 256:384], start=False, stop=True), f"ys{h}")

                        def a1(h):
                            W.wait(MV, f"sc{h ^ 1}", 0 if h else 1)
                            if not h:
                                W.wait(MV, "qh")
                                if c == 0:
                                    W.wait(MG, "vcur")
                                    e.wait_ge(k_in, keys)
                            rows = slice(64 * h, 64 * h + 64)
                            e.matmul(b7[:, 0:128], qh[rows, 0:P], kcur[rows, 0:P], start=True, stop=True)
                            MP.mark(e.matmul(b7[:, 128:384], qh[rows, P:TOK], kcur[rows, :], start=True, stop=True), f"A1_{h}")

                        def a2(h):
                            W.wait(MA, f"pn1{h}")
                            W.wait(MA, f"pt{h ^ 1}", 0 if h else 1)
                            for q in range(3):
                                ins = e.transpose(b5[:, q * P:q * P + P], pr[:, q * P:q * P + P], C("ident"))
                            MP.mark(ins, f"A2_{h}")

                        def a3(h):
                            W.wait(MA, f"pt{h}")
                            W.wait(MV, "yv")
                            rows = slice(64 * h, 64 * h + 64)
                            e.matmul(ps_att[rows, :], vcur[:, 0, :], pt[:, h, 0:256], start=True, stop=False)
                            MP.mark(e.matmul(ps_att[rows, 128:256], vcur[:, 1, :], pt[:, h, 256:384], start=False, stop=True), f"A3_{h}")

                        def halfway(t):
                            def stage(q):
                                if q == 2 and t == 1:
                                    W.wait(MA, "q_sq")
                                    W.wait(MV, "q_s", 1)
                                    W.wait(MV, "sc1", 1)
                                    MP.mark(e.matmul(b7[:, 0:256], C("blk"), tq[:], start=True, stop=True), "q_ss")
                                if q == 2 and t == 4:
                                    a1(1)
                                if q == 2 and t == 3:
                                    W.wait(MV, "qn")
                                    MP.mark(e.matmul(b7[:, 256:512], C("rot"), qn[:], start=True, stop=True), "q_rot")
                                if q == 3 and t == 5:
                                    a2(1)
                            return stage

                        for t in range(6):
                            s = 6 * c + t
                            pair(nb, s, halfway(t))
                            if t == 1:
                                W.wait(MV, "xc")
                                W.wait(MA, "ex1", 1)
                                for a in range(2):
                                    ins = e.transpose(b6[:, a * P:a * P + P], xc[:, a * P:a * P + P], C("ident"))
                                MP.mark(ins, "xT")
                            if t == 2:
                                diff(0)
                            if t == 3:
                                ssd_y(0)
                                a1(0)
                                diff(1)
                            if t == 4:
                                a2(0)
                                ssd_y(1)
                            if t == 5:
                                a3(0)
                                a3(1)
                            if s == 0:
                                bu(0)
                            if s == 3:
                                bu(1)
                            if s == 5:
                                cs(0)
                                bu(2)
                            if s == 7:
                                cs(1)
                            if s == 8:
                                bu(3)
                            if s == 10:
                                cs(2)
                            if s == 11:
                                cs(3)

                W.last_tile(L)
                nb = e.snap(L * N_LAYER + N_SG)
                for n in range(12):
                    if n < 8:
                        pair(nb, n)
                    else:
                        if n == 8:
                            W.wait(LV, "g2_lo")
                        units(nb, n, [(g2_hi, g2_lo)] * 2)
                    if 2 <= n < 6:
                        q = n - 2
                        W.wait(LA, f"ssd_sq{q}")
                        for a in range(2):
                            ins = e.matmul(b4[:, 0:256], C("ones"), ssq[:, q % 2, a * 256:a * 256 + 256],
                                           start=(q == 0 and a == 0), stop=(q == 3 and a == 1))
                        LP.mark(ins, f"ssd_ss{q}")
                sides = [(ys[:, SG:SG + BT, :], ys[:, U:U + BT, :]), (ys[:, XS:XS + BT, :], ys[:, Z:Z + BT, :]),
                         (ys[:, AG:AG + BT, :], ys[:, Q:Q + BT, :])]
                W.wait(MV, "end")
                W.wait(LV, "ssd_lo3")
                W.settle()
                with e.Fori(0, 2) as I:
                    nb = e.snap(L * N_LAYER + N_BR + I * 12)
                    for j in range(12):
                        units(nb, j, [sides[BRANCHES[(2 * j + a) % 3]] for a in range(2)],
                              (lambda: W.wait(LV, "glu_lo3")) if j == 1 else None)
                W.settle()
                with e.Fori(0, 4) as I:
                    nb = e.snap(L * N_LAYER + N_OUT + I * 4)
                    for j in range(4):
                        pair(nb, j, (lambda q: e.wait_ge(merged_lo, e.snap(L * KT + (4 * q + 4)))) if j == 0 else None)

        found = {}
        for k, s in steps.items():
            twice = 2 if k[0] in "MS" else 1
            n = len(s.seen) // twice
            assert s.seen == s.seen[:n] * twice and len(set(s.seen[:n])) == n, k
            assert order is None or s.names == s.seen[:n]
            found[k] = s.seen[:n]
        return found


INPUTS = ("x", "norm_w", "params", "consts", "bdense", "stream")


def lay_out(i):
    f = np.float32

    def tiles(a, n):
        return a.reshape(DEPTH, n, P).transpose(0, 2, 1)

    def states(a):
        return a.reshape(DEPTH, ST, 2, S5_STATE).transpose(0, 2, 3, 1).reshape(DEPTH, P, ST)

    def rows(a):
        return np.broadcast_to(a[:, None, :], (DEPTH, P, a.shape[1]))

    w_in = i["w_in"].reshape(DEPTH, KT, P, -1)
    at = {}
    o = 0
    for n, w in (("u", BW), ("sg", BW), ("z", BW), ("xs", BW), ("bc", 512), ("dt", 16), ("q", BW), ("k", 256), ("v", 256),
                 ("ag", BW), ("gates", 3 * D_MODEL)):
        at[n] = o
        o += w
    par = {
        "a_re": states(i["s5_a_re"]), "a_im": states(i["s5_a_im"]),
        "log_dt": states(np.broadcast_to(i["s5_log_dt"][:, :, None], (DEPTH, S5_GROUPS, S5_STATE))),
        "s5_d": tiles(i["s5_d"], BT), "b_glu": tiles(i["s5_b_glu"], BT),
        "conv": np.concatenate([i["ssd_conv_w"], i["ssd_conv_b"][:, None]], 1).reshape(DEPTH, 5, 12, P).transpose(0, 3, 2, 1)
        .reshape(DEPTH, P, 60),
        "ssd_norm": tiles(i["ssd_norm_w"], BT),
        "ssd_d": tiles(np.repeat(i["ssd_d"], HD, axis=1), BT),
        "q_norm": np.tile(i["att_q_norm"], (1, 2))[:, :, None], "k_norm": np.tile(i["att_k_norm"], (1, 2))[:, :, None],
        "dt_bias": rows(i["ssd_dt_bias"]), "a_log": rows(i["ssd_a_log"]), "sinks": rows(i["att_sinks"]),
        "w_dt": w_in[:, :, :, at["dt"]:at["dt"] + 16].transpose(0, 2, 1, 3).reshape(DEPTH, P, KT * 16),
        "c_re": i["s5_c_re"].reshape(DEPTH, ST, 2, 16, 64).transpose(0, 2, 4, 1, 3).reshape(DEPTH, P, ST * 16),
        "c_im": i["s5_c_im"].reshape(DEPTH, ST, 2, 16, 64).transpose(0, 2, 4, 1, 3).reshape(DEPTH, P, ST * 16),
    }
    params = np.empty((DEPTH, P, NPP), f)
    for n, (a, w) in PP.items():
        params[:, :, a:a + w] = par[n]
    b = np.stack([i["s5_b_re"], i["s5_b_im"]], 3)
    bdense = b.reshape(DEPTH, BT, 8, S5_STATE, 2, S5_GROUP).transpose(0, 1, 2, 5, 4, 3).reshape(DEPTH, BT, P, 2 * S5_STATE)

    stream = np.empty((DEPTH, N_LAYER, P, PAIR), f)

    def full(n, w4, col):
        stream[:, n] = w4[:, :, :, col:col + P].transpose(0, 2, 1, 3).reshape(DEPTH, P, PAIR)

    def unit(n, a, w4, col):
        stream[:, n, :, a * 1024:a * 1024 + 1024] = w4[:, :, :, col:col + P].transpose(0, 2, 1, 3).reshape(DEPTH, P, 1024)

    for m in range(4):
        full(N_BC + m, w_in, at["bc"] + m * P)
    for m in range(2):
        full(N_KV + m, w_in, at["k"] + m * P)
        full(N_KV + 2 + m, w_in, at["v"] + m * P)
    for at_pair, n in ((N_U, "u"), (N_SG, "sg"), (N_IN, "z"), (N_IN + 8, "xs"), (N_IN + 16, "q"), (N_IN + 24, "ag")):
        for m in range(BT):
            full(at_pair + m, w_in, at[n] + m * P)
    for m in range(KT):
        for k, br in enumerate(BRANCHES):
            full(N_GATE + 3 * m + k, w_in, at["gates"] + br * D_MODEL + m * P)
    glu = i["s5_w_glu"].reshape(DEPTH, BT, P, BW)
    for m in range(BT):
        unit(N_GLU + m // 2, m % 2, glu, m * P)
    for m in range(KT):
        for k, br in enumerate(BRANCHES):
            u = 3 * m + k
            unit(N_BR + u // 2, u % 2, i["w_branch"][:, br].reshape(DEPTH, BT, P, D_MODEL), m * P)
    w_out = i["w_out"].reshape(DEPTH, KT, P, D_MODEL)
    for m in range(KT):
        full(N_OUT + m, w_out, m * P)
    stream = stream.reshape(DEPTH * N_LAYER, P, PAIR)
    return {
        "x": np.ascontiguousarray(i["x"][0].T.reshape(KT, P, TOK).transpose(1, 0, 2)),
        "norm_w": np.ascontiguousarray(i["norm_w"].reshape(DEPTH, KT, P).transpose(2, 0, 1)),
        "params": params, "consts": constants(), "bdense": np.ascontiguousarray(bdense),
        "stream": np.concatenate([stream, stream[:RAW]]),
    }


def declare(nc, arrays):
    args = [nc.dram_tensor(f"in_{n}", arrays[n].shape, F32, kind="ExternalInput").ap() for n in INPUTS]
    return args + [nc.dram_tensor("out_0", (DEPTH + 1, P, KT, TOK), F32, kind="ExternalOutput").ap()]


def kernel(**inputs):
    import concourse.bacc as _bacc
    from concourse.bass_utils import run_bass_kernel_spmd as _run

    arrays = lay_out({k: np.asarray(v) for k, v in inputs.items()})
    order = None
    for _ in range(2):
        nc = _bacc.Bacc("TRN2", target_bir_lowering=False, num_devices=1)
        order = program(nc, *declare(nc, arrays), order)
    r = _run(nc, [{f"in_{n}": arrays[n] for n in INPUTS}], core_ids=[0])
    y = r.results[0]["out_0"][DEPTH]
    return np.ascontiguousarray(y.transpose(1, 0, 2).reshape(D_MODEL, TOK).T)[None]
```
